# Optimizing a Trainium2 kernel written in Bass

```python
import jax, jax.numpy as jnp
from jax import lax
import numpy as np

D_MODEL = 1024
BATCH = 1
SEQ = 256
DEPTH = 2

N_A_LAYERS = max(1, DEPTH // 2)
N_B_LAYERS = DEPTH - N_A_LAYERS

D_RNN = D_MODEL
N_RG_BLOCKS = 8
RG_BW = D_RNN // N_RG_BLOCKS
CONV_WIDTH = 4
RG_C = 8.0

N_HEADS = 8
HEAD_DIM = 128
D_ATTN = N_HEADS * HEAD_DIM
MOBA_BLOCK = 256
MOBA_TOPK = 3
Q_CHUNK = 64
ROPE_THETA = 10000.0
EPS = 1e-6
NEG_INF = -1e30

kernel_name = "hawk_moba_yoco_hybrid"

def rms_norm(x, g):
    xf = x.astype(jnp.float32)
    y = xf * lax.rsqrt(jnp.mean(xf * xf, axis=-1, keepdims=True) + EPS)
    return (y * g.astype(jnp.float32)).astype(x.dtype)

def rope(x, pos):
    half = HEAD_DIM // 2
    inv = ROPE_THETA ** (-jnp.arange(half, dtype=jnp.float32) / half)
    ang = pos.astype(jnp.float32)[:, None] * inv[None, :]
    cos = jnp.cos(ang)[None, :, None, :]
    sin = jnp.sin(ang)[None, :, None, :]
    xf = x.astype(jnp.float32)
    x1, x2 = xf[..., :half], xf[..., half:]
    return jnp.concatenate([x1 * cos - x2 * sin, x2 * cos + x1 * sin], axis=-1).astype(x.dtype)

def causal_depthwise_conv(x, w, b):
    S = x.shape[1]
    xp = jnp.pad(x, ((0, 0), (CONV_WIDTH - 1, 0), (0, 0)))
    y = xp[:, 0:S] * w[0]
    for k in range(1, CONV_WIDTH):
        y = y + xp[:, k:k + S] * w[k]
    return y + b

def block_diag_linear(x, w, b):
    B, S, _ = x.shape
    xb = x.reshape(B, S, N_RG_BLOCKS, RG_BW)
    y = jnp.einsum('bsni,nij->bsnj', xb, w).reshape(B, S, D_RNN)
    return y + b

def rg_lru(x, r_w, r_b, i_w, i_b, lam):
    r = jax.nn.sigmoid(block_diag_linear(x, r_w, r_b).astype(jnp.float32))
    i = jax.nn.sigmoid(block_diag_linear(x, i_w, i_b).astype(jnp.float32))
    log_a = -RG_C * r * jax.nn.softplus(-lam.astype(jnp.float32))
    a = jnp.exp(log_a)
    mult = jnp.sqrt(-jnp.expm1(2.0 * log_a))
    bterm = mult * (i * x.astype(jnp.float32))

    def combine(left, right):
        a_l, b_l = left
        a_r, b_r = right
        return a_l * a_r, a_r * b_l + b_r

    _, h = lax.associative_scan(combine, (a, bterm), axis=1)
    return h.astype(x.dtype)

def hawk_layer(x, norm_g, in_w, conv_w, conv_b, r_w, r_b, i_w, i_b, lam, out_w):
    h = rms_norm(x, norm_g)
    u = h @ in_w
    xb, gate = u[..., :D_RNN], u[..., D_RNN:]
    xb = causal_depthwise_conv(xb, conv_w, conv_b)
    y = rg_lru(xb, r_w, r_b, i_w, i_b, lam) * jax.nn.silu(gate)
    return x + y @ out_w

def shared_kv(x, kv_norm_g, kv_w, k_norm_g, pos):
    B, S, _ = x.shape
    h = rms_norm(x, kv_norm_g)
    kv = (h @ kv_w).reshape(B, S, 2, N_HEADS, HEAD_DIM)
    k = rope(rms_norm(kv[:, :, 0], k_norm_g), pos)
    v = kv[:, :, 1]
    nb = -(-S // MOBA_BLOCK)
    pad = nb * MOBA_BLOCK - S
    k = jnp.pad(k, ((0, 0), (0, pad), (0, 0), (0, 0)))
    v = jnp.pad(v, ((0, 0), (0, pad), (0, 0), (0, 0)))
    kb = k.reshape(B, nb, MOBA_BLOCK, N_HEADS, HEAD_DIM).transpose(0, 3, 1, 2, 4)
    vb = v.reshape(B, nb, MOBA_BLOCK, N_HEADS, HEAD_DIM).transpose(0, 3, 1, 2, 4)
    kmean = jnp.mean(kb.astype(jnp.float32), axis=3)
    return kb, vb, kmean

def moba_attention(q, kb, vb, kmean):
    B, S, H, Dh = q.shape
    nb = kb.shape[2]
    topk = min(MOBA_TOPK, nb)
    qh = jnp.transpose(q, (0, 2, 1, 3))
    scale = HEAD_DIM ** -0.5
    blk_ids = jnp.arange(nb)
    gather_blocks = jax.vmap(jax.vmap(lambda t, idx: t[idx]))

    def chunk(c):
        q0 = c * Q_CHUNK
        qc = lax.dynamic_slice_in_dim(qh, q0, Q_CHUNK, axis=2)
        qpos = q0 + jnp.arange(Q_CHUNK)
        own = q0 // MOBA_BLOCK
        g = jnp.einsum('bhqd,bhnd->bhqn', qc.astype(jnp.float32), kmean)
        g = jnp.where(blk_ids < own, g, -jnp.inf)
        _, sel = lax.top_k(g, topk)
        valid = sel < own
        k_sel = gather_blocks(kb, sel)
        v_sel = gather_blocks(vb, sel)
        s_sel = jnp.einsum('bhqd,bhqkld->bhqkl', qc, k_sel).astype(jnp.float32) * scale
        s_sel = jnp.where(valid[..., None], s_sel, NEG_INF)
        k_own = lax.dynamic_index_in_dim(kb, own, axis=2, keepdims=False)
        v_own = lax.dynamic_index_in_dim(vb, own, axis=2, keepdims=False)
        s_own = jnp.einsum('bhqd,bhld->bhql', qc, k_own).astype(jnp.float32) * scale
        kpos = own * MOBA_BLOCK + jnp.arange(MOBA_BLOCK)
        s_own = jnp.where(kpos[None, :] <= qpos[:, None], s_own, NEG_INF)
        s = jnp.concatenate([s_sel.reshape(B, H, Q_CHUNK, topk * MOBA_BLOCK), s_own], axis=-1)
        p = jax.nn.softmax(s, axis=-1).astype(q.dtype)
        p_sel = p[..., :topk * MOBA_BLOCK].reshape(B, H, Q_CHUNK, topk, MOBA_BLOCK)
        p_own = p[..., topk * MOBA_BLOCK:]
        return (jnp.einsum('bhqkl,bhqkld->bhqd', p_sel, v_sel)
                + jnp.einsum('bhql,bhld->bhqd', p_own, v_own))

    o = lax.map(chunk, jnp.arange(S // Q_CHUNK))
    return jnp.transpose(o, (1, 0, 3, 2, 4)).reshape(B, S, H * Dh)

def moba_layer(x, norm_g, in_w, q_norm_g, out_w, kb, vb, kmean, pos):
    B, S, _ = x.shape
    h = rms_norm(x, norm_g)
    u = h @ in_w
    q = u[..., :D_ATTN].reshape(B, S, N_HEADS, HEAD_DIM)
    gate = u[..., D_ATTN:]
    q = rope(rms_norm(q, q_norm_g), pos)
    o = moba_attention(q, kb, vb, kmean) * jax.nn.silu(gate)
    return x + o @ out_w

def setup_inputs(seed: int = 0) -> dict:
    key = jax.random.key(seed)
    ks = jax.random.split(key, 24)
    f32 = jnp.float32
    nA, nB = N_A_LAYERS, N_B_LAYERS

    def nrm(k, shape, scale):
        return jax.random.normal(k, shape, f32) * scale

    x = jax.random.normal(ks[0], (BATCH, SEQ, D_MODEL), f32)
    a_norm = 1.0 + nrm(ks[1], (nA, D_MODEL), 0.02)
    a_in_w = nrm(ks[2], (nA, D_MODEL, 2 * D_RNN), D_MODEL ** -0.5)
    a_conv_w = nrm(ks[3], (nA, CONV_WIDTH, D_RNN), CONV_WIDTH ** -0.5)
    a_conv_b = nrm(ks[4], (nA, D_RNN), 0.02)
    a_r_w = nrm(ks[5], (nA, N_RG_BLOCKS, RG_BW, RG_BW), RG_BW ** -0.5)
    a_r_b = nrm(ks[6], (nA, D_RNN), 0.02)
    a_i_w = nrm(ks[7], (nA, N_RG_BLOCKS, RG_BW, RG_BW), RG_BW ** -0.5)
    a_i_b = nrm(ks[8], (nA, D_RNN), 0.02)
    a_c = jax.random.uniform(ks[9], (nA, D_RNN), f32, 0.9, 0.999)
    a_base = a_c ** (1.0 / RG_C)
    a_lambda = jnp.log(a_base) - jnp.log1p(-a_base)
    a_out_w = nrm(ks[10], (nA, D_RNN, D_MODEL), D_RNN ** -0.5)
    kv_norm = 1.0 + nrm(ks[11], (D_MODEL,), 0.02)
    kv_w = nrm(ks[12], (D_MODEL, 2 * D_ATTN), D_MODEL ** -0.5)
    k_norm = 1.0 + nrm(ks[13], (HEAD_DIM,), 0.02)
    b_norm = 1.0 + nrm(ks[14], (nB, D_MODEL), 0.02)
    b_in_w = nrm(ks[15], (nB, D_MODEL, 2 * D_ATTN), D_MODEL ** -0.5)
    q_norm = 1.0 + nrm(ks[16], (nB, HEAD_DIM), 0.02)
    b_out_w = nrm(ks[17], (nB, D_ATTN, D_MODEL), D_ATTN ** -0.5)
    return {"x": x, "a_norm": a_norm, "a_in_w": a_in_w, "a_conv_w": a_conv_w, "a_conv_b": a_conv_b,
            "a_r_w": a_r_w, "a_r_b": a_r_b, "a_i_w": a_i_w, "a_i_b": a_i_b, "a_lambda": a_lambda,
            "a_out_w": a_out_w, "kv_norm": kv_norm, "kv_w": kv_w, "k_norm": k_norm,
            "b_norm": b_norm, "b_in_w": b_in_w, "q_norm": q_norm, "b_out_w": b_out_w}

def reference(x, a_norm, a_in_w, a_conv_w, a_conv_b, a_r_w, a_r_b, a_i_w, a_i_b, a_lambda,
              a_out_w, kv_norm, kv_w, k_norm, b_norm, b_in_w, q_norm, b_out_w):
    S = x.shape[1]
    pos = jnp.arange(S, dtype=jnp.int32)
    for l in range(N_A_LAYERS):
        x = hawk_layer(x, a_norm[l], a_in_w[l], a_conv_w[l], a_conv_b[l], a_r_w[l], a_r_b[l],
                       a_i_w[l], a_i_b[l], a_lambda[l], a_out_w[l])
    kb, vb, kmean = shared_kv(x, kv_norm, kv_w, k_norm, pos)
    for j in range(N_B_LAYERS):
        x = moba_layer(x, b_norm[j], b_in_w[j], q_norm[j], b_out_w[j], kb, vb, kmean, pos)
    return x


_drawn_inputs = setup_inputs


def setup_inputs(seed=0):
    import zlib

    import numpy as np

    out = dict(_drawn_inputs(seed))
    spreads = {}
    factors = {'a_norm': 6.02,
     'a_r_b': 8.0,
     'a_i_b': 8.0,
     'kv_norm': 8.0,
     'k_norm': 8.0,
     'b_norm': 8.0,
     'q_norm': 8.0}
    for name, (base, spread) in spreads.items():
        noise = np.random.default_rng([zlib.crc32(name.encode()), seed]).standard_normal(out[name].shape)
        drawn = base * np.exp(spread * noise) if base else spread * noise
        out[name] = __import__('jax').numpy.asarray(drawn.astype(out[name].dtype))
    for name, factor in factors.items():
        out[name] = (out[name] * factor).astype(out[name].dtype)
    return out
```

```python
from contextlib import ExitStack

import concourse.bass as bass
from concourse import mybir

P = 128
F32 = mybir.dt.float32
F32R = mybir.dt.float32r
BF16 = mybir.dt.bfloat16
ALU = mybir.AluOpType
ACT = mybir.ActivationFunctionType
AX_X = mybir.AxisListType.X
EPS = 1e-6
NEG_INF = -1e30
RG_C = 8.0

VECTORS = ["conv_w0", "conv_w1", "conv_w2", "conv_w3", "conv_b", "r_b", "i_b", "lambda", "a_norm", "kv_norm", "b_norm"]


def hybrid_trunk(nc, xT, x, in_w, r_w, i_w, a_out_w, kv_w, b_in_w, b_out_w, vectors, head_norms, rope_cs, identity, y):
    D, S = xT.shape
    KT = D // P
    TT = S // P
    NB = r_w.shape[0]
    CH = 512
    UK = 2
    UPC = KT // UK
    DH = P
    H = D // DH
    HG = CH // DH
    SCALE = float(DH) ** -0.5
    assert D == 1024 and S == 256 and NB == KT and in_w.shape[1] == 2 * D

    def cols(w, c):
        return w[:, c * CH:(c + 1) * CH]

    CHUNKS = [(cols(in_w, c), None) for c in range(4)]
    CHUNKS += [(cols(a_out_w, c), None) for c in range(2)]
    CHUNKS += [(cols(kv_w, 0), "kv_norm"), (cols(b_in_w, 0), "b_norm"), (cols(kv_w, 2), "kv_norm")]
    CHUNKS += [(cols(kv_w, 1), "kv_norm"), (cols(b_in_w, 1), "b_norm"), (cols(kv_w, 3), "kv_norm")]
    CHUNKS += [(cols(b_in_w, 2), "b_norm"), (cols(b_in_w, 3), "b_norm")]
    CHUNKS += [(cols(b_out_w, c), None) for c in range(2)]
    KINDS = ["k", "q", "v", "k", "q", "v", "g", "g"]
    HALF = [0, 0, 0, 1, 1, 1, 0, 1]
    C_OUT_A, C_B, C_OUT_B = 4, 6, 14
    NU = len(CHUNKS) * UPC
    Y_PARTS = [(0, 0, CH), (1, 0, CH), (2, 0, CH), (3, 0, CH // 2), (3, CH // 2, CH)]
    GATES_AT = {3: {1: 0}, 4: {6: 1}, 5: {0: 2}, 6: {2: 3}, 7: {2: 4, 7: 5}, 8: {6: 6}, 9: {4: 7}}
    X1_TURN_AT = {(2, 1): 0, (2, 2): 1, (3, 5): 2}
    WARM = 9
    RAW = 4
    WR = 3

    def unit(u):
        c, n = u // UPC, u % UPC
        if c == 0:
            k0, c0 = n % 2 * 2 * UK, n // 2 * (CH // 2)
            return c, slice(k0, k0 + 2 * UK), slice(c0, c0 + CH // 2)
        return c, slice(n * UK, (n + 1) * UK), slice(0, CH)

    SPLIT_X = [[], [4], [5, 6, 7], [], [8], [9], [10], [11]]
    ACT_G = ("12 13 gates:6 gates:7 14 15 16 sqrt silu:0 silu:1 silu:2 17 silu:3 silu:4 18 mix:0 19 silu:5 mix:1 "
             "silu:6 mix:2 silu:7 20 mix:3")
    DVE_G = ("12 13 ia:0 ix:5 ix:6 ix:7 zs:0 ia:1 ia:2 zs:1 ia:3 ia:4 ia:5 ia:6 14 15 zs:2 16 zs:3 ia:7 scan:0 "
             "scan:1 scan:2 scan:3 mix:0 mix:1 zs:4 scan:4 17 mix:2 mix:3 scan:5 18 zs:5 lo:0 scan:6 scan:7 19 "
             "mix:4 lo:1 zs:6 zs:7 mix:5 mix:6 mix:7 lo:2 20 lo:3")
    ACT_O = "21 22 23 sq:0 sq:1 xT:0 xT:1 24 25 26 27 sq:2 28 xT:2 29 sq:3 30 xT:3 rms1"
    DVE_O = "21 22 23 x1:0 x1:1 xT:0 xT:1 24 25 x1:2 26 27 28 xT:2 x1:3 29 30 xT:3 rms1"
    PE_B = {(3, 6): ["kqT 0"], (5, 0): ["kqT 1"], (5, 7): ["scores 0", "scores 1"], (6, 3): ["pT 0"],
            (6, 5): ["scores 2", "pT 1"], (6, 7): ["pv 0"], (7, 2): ["scores 3"], (7, 6): ["pv 1"],
            (8, 0): ["pT 2"], (8, 4): ["pT 3"], (8, 6): ["pv 2"], (9, 0): ["pv 3"], (9, 4): ["kqT 2"],
            (11, 2): ["kqT 3"], (11, 4): ["scores 4", "scores 5"], (12, 3): ["pT 4"],
            (12, 4): ["scores 6", "pT 5"], (13, 0): ["pv 4", "scores 7"], (13, 2): ["pT 6"], (13, 3): ["pv 5"],
            (13, 4): ["pT 7"], (13, 6): ["pv 6"], (14, 2): ["pv 7"], (14, 3): ["oT 0"], (14, 6): ["oT 1"],
            (16, 0): ["oT 2"], (16, 5): ["oT 3"]}
    ACT_B = ("31 out:0 32 33 out:1 34 rms:0 out:2 35 36 out:3 rms:1 37 kqT:0 38 39 40 out:4 kqT:1 exp:0 out:5 exp:1 "
             "41 42 out:6 43 exp:2 exp:3 out:7 rms:2 44 out:8 45 46 47 out:9 kqT:2 rms:3 48 49 out:10 kqT:3 50 "
             "exp:4 out:11 exp:5 51 52 exp:6 exp:7 out:12 53 54 55 out:13 oT:0 56 57 oT:1 out:14 58 59 60 oT:2 "
             "out:15 61 oT:3 62 63")
    DVE_B = ("31 out:0 32 33 ms:0 out:1 34 norm:0 out:2 35 36 ms:1 out:3 norm:1 37 38 39 40 max:0 max:1 41 probT:0 "
             "42 max:2 probT:1 max:3 43 out:6 probT:2 ms:2 attend:0 out:7 probT:3 norm:2 attend:1 44 45 out:8 46 47 "
             "ms:3 out:9 norm:3 48 49 50 max:4 max:5 51 probT:4 max:6 probT:5 52 max:7 gate:0 probT:6 attend:2 53 "
             "54 probT:7 55 gate:1 56 attend:3 oT:0 57 gate:2 oT:1 58 59 oT:2 gate:3 60 oT:3 61 62 63")

    def steps_of(text):
        for word in text.split():
            name, _, arg = word.partition(":")
            yield ("split", int(name)) if name.isdecimal() else (name, int(arg) if arg else None)

    with ExitStack() as ctx:
        def sb(name, shape, dt=F32):
            return ctx.enter_context(nc.sbuf_tensor(name, shape, dt))

        def sem(name):
            return ctx.enter_context(nc.semaphore(name))

        raw = sb("raw", [P, RAW, UK * CH])
        w_hi = sb("w_hi", [P, WR, KT, CH], F32R)
        w_lo = sb("w_lo", [P, WR, KT, CH], F32R)
        act_hi = sb("act_hi", [P, KT, S], F32R)
        act_lo = sb("act_lo", [P, KT, S], F32R)
        mix_hi = sb("mix_hi", [P, KT, S], F32R)
        mix_lo = sb("mix_lo", [P, KT, S], F32R)
        buf = [sb(f"buf{n}", [P, KT * S]) for n in range(5)]
        scratch = sb("scratch", [P, 2560])
        rope_t = sb("rope_t", [P, 4, TT, DH])
        ident = sb("ident", [P, P])
        ident_b = sb("ident_b", [P, P], BF16)
        mask_b = sb("mask_b", [P, P], BF16)
        ones = sb("ones", [P, P])
        head_norm = sb("head_norm", [P, 2, DH])
        rope_b = sb("rope_b", [P, TT * CH])
        vec = sb("vec", [P, len(VECTORS), KT])
        lru = sb("lru", [P, 8, KT])
        small = sb("small", [P, 160])

        def ch3(t):
            return t[:, :].rearrange("p (k s) -> p k s", k=KT)

        def tok3(t):
            return t[:, :].rearrange("p (t c) -> p t c", t=TT)

        xT_sb, decay = ch3(buf[0]), ch3(buf[0])
        conv, zs, mix = ch3(buf[1]), ch3(buf[1]), ch3(buf[1])
        rgate, state = ch3(buf[2]), ch3(buf[2])
        xs, igate, silu_z = ch3(buf[3]), ch3(buf[3]), ch3(buf[3])
        square, drive = ch3(buf[4]), ch3(buf[4])
        ms0, y0, t0, rstd0 = (rope_b[:, n * S:(n + 1) * S] for n in range(4))
        rw = scratch[:, 0:NB * P].rearrange("p (n j) -> p n j", n=NB)
        iw = scratch[:, NB * P:2 * NB * P].rearrange("p (n j) -> p n j", n=NB)
        x1 = tok3(buf[0])
        roped = [tok3(buf[1])[:, 0], rope_b[:, :]]
        roped = [r.rearrange("p (t c) -> p t c", t=TT) for r in roped]
        att = [tok3(buf[1])[:, 1], tok3(buf[1])[:, 0]]
        att = [r.rearrange("p (t c) -> p t c", t=TT) for r in att]
        value = tok3(buf[2])
        y_sb = buf[2][:, :].rearrange("p (i c) -> p i c", c=CH)
        keyT = ch3(buf[3])
        x_sb, queryT = tok3(buf[4]), ch3(buf[4])
        sq_sb = scratch[:, 0:CH]
        swap_sb = scratch[:, CH:2 * CH]
        gate = scratch[:, 0:2 * CH].rearrange("p (r c) -> p r c", r=2)
        prob = scratch[:, 1024:1024 + 768].rearrange("p (r c) -> p r c", r=2)
        probT = scratch[:, 1792:1792 + 768].rearrange("p (r c) -> p r c", r=2)

        def raw_unit(u):
            _, ks, cs = unit(u)
            return raw[:, u % RAW].rearrange("p (k c) -> p k c", c=cs.stop - cs.start)

        def V(name):
            return vec[:, VECTORS.index(name), :]

        decay_half, decay_neg, rb_half, ib_half = lru[:, 0, :], lru[:, 1, :], lru[:, 2, :], lru[:, 3, :]
        ssq = small[:, 0:4].rearrange("p (t d) -> p t d", t=TT)
        ms1, rstd1, nt1 = (small[:, 4 + 2 * n:6 + 2 * n] for n in range(3))
        ssk = small[:, 12:20]
        msk, nyk, ntk = small[:, 20:28], small[:, 28:36], small[:, 36:44]
        q_scale = small[:, 44:60].rearrange("p (t h) -> p t h", t=TT)
        q_nscale = small[:, 60:76].rearrange("p (t h) -> p t h", t=TT)
        smax = small[:, 76:92].rearrange("p (t h) -> p t h", t=TT)
        nbias = small[:, 92:108].rearrange("p (t h) -> p t h", t=TT)
        psum_l = small[:, 108:124].rearrange("p (h t) -> p h t", t=TT)
        recip_l = small[:, 124:140].rearrange("p (h t) -> p h t", t=TT)

        bank = [ctx.enter_context(nc.psum_tensor(f"bank{n}", [P, 512], F32)) for n in range(8)]

        xT_in = [sem(f"xT_in{n}") for n in range(UPC)]
        x_in, vec_in, gate_w_in, table_in, ident_in = (sem(n) for n in ("x_in", "vec_in", "gate_w_in", "table_in", "ident_in"))
        raw_in = [sem(f"raw_in{n}") for n in range(RAW)]
        out_done = sem("out_done")
        hi_done, lo_done = sem("hi_done"), sem("lo_done")
        const_made, lru_made, table_made = sem("const_made"), sem("lru_made"), sem("table_made")
        pool_step = sem("pool_step")
        lam_exp, lam_abs = sem("lam_exp"), sem("lam_abs")
        squared, stat_done, ms0_done, y0_done, rstd0_done = (sem(n) for n in ("squared", "stat_done", "ms0_done", "y0_done", "rstd0_done"))
        hhi_done, hlo_done = sem("x_hi_done"), sem("x_lo_done")
        xs_done, zs_done = sem("xs_done"), sem("zs_done")
        x_done, ri_done, g_done = sem("x_done"), sem("ri_done"), sem("g_done")
        tap0_done, conv_done = sem("tap0_done"), sem("conv_done")
        gates_done, decay_done = sem("gates_done"), sem("decay_done")
        ix_done, ia_done, m_done = sem("ix_done"), sem("ia_done"), sem("m_done")
        b_done, scan_done, silu_done, mix_done = (sem(n) for n in ("b_done", "scan_done", "silu_done", "mix_done"))
        mhi_done, mlo_done = sem("mix_hi_done"), sem("mix_lo_done")
        o_done, x1_done, x1sq_done = sem("out_a_done"), sem("x1_done"), sem("x1sq_done")
        xt_done, xhi_done, xlo_done = sem("x1T_done"), sem("x1T_hi"), sem("x1T_lo")
        ms1_done, y1_done, rstd1_done = sem("ms1_done"), sem("y1_done"), sem("rstd1_done")
        u_done = sem("u_done")
        sq_done, cos_done, kq_done = sem("sq_done"), sem("cos_done"), sem("kq_done")
        msk_done, yk_done = sem("msk_done"), sem("yk_done")
        t_done, tcopy_done, v_done = sem("kqT_done"), sem("kqT_copied"), sem("v_done")
        s_done, nb_done, p_done, pt_done, ptc_done = (sem(n) for n in ("s_done", "nb_done", "p_done", "pt_done", "pt_copied"))
        pv_done, on_done = sem("pv_done"), sem("on_done")
        gate_done, og_done, ot_done = sem("gate_done"), sem("og_done"), sem("ot_done")
        f_done, y_done = sem("f_done"), sem("y_done")
        add_done = sem("add_done")
        dve_step = sem("dve_step")

        def earlier(n, kinds):
            return sum(KINDS[j // TT] in kinds for j in range(n))

        O_BANKS = [6, 7, 3, 2]

        def acc_free(n):
            if n < 2:
                return zs_done, 4 + n + 1
            if n == 2:
                return x1_done, 4
            m = n - 3
            kind = KINDS[m // 2]
            if kind in "kq":
                return cos_done, earlier(m + 1, "kq")
            return (v_done if kind == "v" else gate_done), earlier(m + 1, kind)

        def y_bank(i, c0):
            return bank[(16 + i + (c0 > 0)) % 3]

        TURNS = [("x1T", i, xlo_done, i + 1) for i in range(4)]
        TURNS += [("kqT", i, tcopy_done, i + 1) for i in range(4)]
        TURNS += [("pT", h, ptc_done, h + 1) for h in range(4)]
        TURNS += [("kqT", i, tcopy_done, i + 1) for i in range(4, 8)]
        TURNS += [("pT", h, ptc_done, h + 1) for h in range(4, 8)]
        TURNS += [("oT", i, mlo_done, NB // 2 + i + 1) for i in range(4)]
        TURN = {(what, i): n for n, (what, i, _, _) in enumerate(TURNS)}

        def turn_bank(what, i):
            return bank[4 + TURN[(what, i)] % 2]

        def turn_free(what, i):
            n = TURN[(what, i)]
            if n < 2:
                return gates_done, 2 * NB
            return TURNS[n - 2][2], TURNS[n - 2][3]

        block = ctx.enter_context(nc.Block())

        @block.sync
        def _(sp):
            def load(u):
                if u >= RAW:
                    sp.wait_ge(lo_done, u - RAW + 1)
                c, ks, cs = unit(u)
                w = CHUNKS[c][0][ks.start * P:ks.stop * P, cs].rearrange("(k p) c -> p k c", p=P)
                sp.dma_start(raw_unit(u), w).then_inc(raw_in[u % RAW], 16)

            sp.dma_start(vec[:, :, :], vectors).then_inc(vec_in, 16)
            xT_v = xT.rearrange("(k p) s -> p k s", p=P)
            for n in range(UPC):
                sp.dma_start(xT_sb[:, n * UK:(n + 1) * UK, :], xT_v[:, n * UK:(n + 1) * UK, :]).then_inc(xT_in[n], 16)
                if n % 2 == 0:
                    load(n // 2)
            for u in (2, 3):
                load(u)
            sp.dma_start(rw, r_w.rearrange("n i j -> i n j")).then_inc(gate_w_in, 16)
            sp.dma_start(iw, i_w.rearrange("n i j -> i n j")).then_inc(gate_w_in, 16)
            sp.dma_start(ident[:, :], identity).then_inc(ident_in, 16)
            for n in range(4):
                sp.dma_start(rope_t[:, n], rope_cs[n % 2]).then_inc(table_in, 16)
            for n in range(2):
                sp.dma_start(head_norm[:, n], head_norms[n, :].partition_broadcast(P)).then_inc(table_in, 16)
            for u in range(RAW, NU):
                load(u)
                if u == C_B * UPC - 1:
                    sp.wait_ge(b_done, NB)
                    sp.dma_start(x_sb, x.rearrange("(t p) c -> p t c", p=P)).then_inc(x_in, 16)
            for n, (i, c0, c1) in enumerate(Y_PARTS):
                t, d = i % TT, i // TT
                sp.wait_ge(y_done, n + 1)
                sp.dma_start(y[t * P:(t + 1) * P, d * CH + c0:d * CH + c1], y_sb[:, i, c0:c1]).then_inc(out_done, 16)
            sp.wait_ge(out_done, 16 * len(Y_PARTS))

        def heads(ap):
            return ap.rearrange("p (h d) -> p h d", d=DH)

        def chunk_free(c):
            if c < 2:
                return x_done, 4 * (c + 1)
            if c < C_OUT_A:
                return g_done, 4 * (c - 1)
            if c < C_B:
                return o_done, 2 * (c - C_OUT_A + 1)
            return u_done, 2 * (c - C_B + 1)

        @block.gpsimd
        def _(pool):
            nc.gpsimd.memset(ones[:, :], 1.0).then_inc(const_made, 1)
            nc.gpsimd.memset(mask_b[:, :], 0.0).then_inc(pool_step, 1)
            pool.wait_ge(pool_step, 1)
            nc.gpsimd.affine_select(out=mask_b[:, :], in_=mask_b[:, :], compare_op=ALU.is_ge, fill=NEG_INF, base=0,
                                    pattern=[[-1, P]], channel_multiplier=1).then_inc(const_made, 1)
            pool.wait_ge(ident_in, 16)
            nc.gpsimd.tensor_copy(ident_b[:, :], ident[:, :]).then_inc(const_made, 1)
            pool.wait_ge(table_in, 16 * 6)
            half = DH // 2
            for n in range(2):
                for t in range(TT):
                    nc.gpsimd.tensor_tensor(rope_t[:, 2 * n, t, :], rope_t[:, 2 * n, t, :], head_norm[:, n], ALU.mult)
                    nc.gpsimd.tensor_tensor(rope_t[:, 2 * n + 1, t, 0:half], rope_t[:, 2 * n + 1, t, 0:half],
                                            head_norm[:, n, half:DH], ALU.mult)
                    nc.gpsimd.tensor_tensor(rope_t[:, 2 * n + 1, t, half:DH], rope_t[:, 2 * n + 1, t, half:DH],
                                            head_norm[:, n, 0:half], ALU.mult).then_inc(table_made, 1)
            for b in range(NB):
                pool.wait_ge(m_done, b // 2 + 1)
                pool.wait_ge(ia_done, b + 1)
                nc.gpsimd.tensor_tensor(igate[:, b, :], igate[:, b, :], drive[:, b, :], ALU.mult).then_inc(b_done, 1)

        @block.scalar
        def _(act):
            def split_hi(u):
                c, ks, cs = unit(u)
                act.wait_ge(raw_in[u % RAW], 16 * (u // RAW + 1))
                if c >= WR:
                    act.wait_ge(*chunk_free(c - WR))
                gamma = CHUNKS[c][1]
                if gamma is None:
                    nc.scalar.activation(w_hi[:, c % WR, ks, cs], raw_unit(u), ACT.Copy).then_inc(hi_done, 1)
                else:
                    for k in range(UK):
                        last = nc.scalar.activation(w_hi[:, c % WR, ks.start + k, :], raw_unit(u)[:, k], ACT.Copy,
                                                    scale=V(gamma)[:, ks.start + k:ks.start + k + 1])
                    last.then_inc(hi_done, 1)

            def inv_sqrt(ready, count, ms, out, done):
                act.wait_ge(ready, count)
                nc.scalar.activation(out, ms, ACT.Ln).then_inc(done, 1)
                act.wait_ge(done, 2 * count - 1)
                nc.scalar.activation(out, out, ACT.Exp, scale=-0.5).then_inc(done, 1)

            nc.scalar.preload_act_table_set("natural_log_exp_and_others")
            act.wait_ge(lam_abs, 1)
            nc.scalar.activation(lru[:, 5, :], lru[:, 4, :], ACT.Exp, scale=-1.0).then_inc(lam_exp, 1)
            for n in range(UPC):
                act.wait_ge(xT_in[n], 16)
                for k in (2 * n, 2 * n + 1):
                    last = nc.scalar.activation(act_hi[:, k, :], xT_sb[:, k, :], ACT.Copy, scale=V("a_norm")[:, k:k + 1])
                last.then_inc(hhi_done, 1)
                nc.scalar.activation(square[:, n * UK:(n + 1) * UK, :], xT_sb[:, n * UK:(n + 1) * UK, :], ACT.Square).then_inc(squared, 1)
                if n % 2 == 0:
                    split_hi(n // 2)
            split_hi(2)
            split_hi(3)
            inv_sqrt(ms0_done, 1, ms0, y0, y0_done)
            nc.scalar.preload_act_table_set("exp_and_others")

            def gates(b):
                pri = bank[4 + b % 2]
                act.wait_ge(ri_done, b + 1)
                if b == 0:
                    act.wait_ge(lru_made, 1)
                nc.scalar.activation(rgate[:, b, :], pri[:, 0:S], ACT.Tanh, scale=0.5, bias=rb_half[:, b:b + 1]).then_inc(gates_done, 1)
                nc.scalar.activation(igate[:, b, :], pri[:, S:2 * S], ACT.Tanh, scale=0.5, bias=ib_half[:, b:b + 1]).then_inc(gates_done, 1)
                act.wait_ge(gates_done, 2 * b + 1)
                nc.scalar.activation(decay[:, b, :], rgate[:, b, :], ACT.Exp, scale=decay_half[:, b:b + 1],
                                     bias=decay_half[:, b:b + 1]).then_inc(decay_done, 1)
                nc.scalar.activation(drive[:, b, :], rgate[:, b, :], ACT.Tanh, scale=decay_neg[:, b:b + 1],
                                     bias=decay_neg[:, b:b + 1]).then_inc(decay_done, 1)

            def mix_part_hi(p):
                act.wait_ge(mix_done, 2 * p + 2)
                nc.scalar.activation(mix_hi[:, 2 * p:2 * p + 2, :], mix[:, 2 * p:2 * p + 2, :], ACT.Copy).then_inc(mhi_done, 1)

            def x1T_hi(i):
                t, d = i % TT, i // TT
                act.wait_ge(xt_done, i + 1)
                nc.scalar.activation(act_hi[:, 4 * d:4 * d + 4, t * P:(t + 1) * P], heads(turn_bank("x1T", i)[:, :]),
                                     ACT.Copy).then_inc(xhi_done, 1)

            for b in range(NB):
                for u in SPLIT_X[b]:
                    split_hi(u)
                act.wait_ge(xs_done, b + 1)
                nc.scalar.activation(conv[:, b, :], xs[:, b, :], ACT.Identity, scale=V("conv_w3")[:, b:b + 1],
                                     bias=V("conv_b")[:, b:b + 1]).then_inc(tap0_done, 1)
                if b >= 2:
                    gates(b - 2)
            def sqrt_parts(_):
                act.wait_ge(decay_done, 2 * NB)
                for p in range(NB // 2):
                    nc.scalar.activation(drive[:, 2 * p:2 * p + 2, :], drive[:, 2 * p:2 * p + 2, :], ACT.Sqrt, scale=0.25).then_inc(m_done, 1)
                nc.scalar.preload_act_table_set("silu_and_others")

            def silu_gate(b):
                act.wait_ge(zs_done, b + 1)
                act.wait_ge(scan_done, b + 1)
                nc.scalar.activation(silu_z[:, b, :], zs[:, b, :], ACT.Silu).then_inc(silu_done, 1)

            for what, arg in steps_of(ACT_G):
                {"split": split_hi, "gates": gates, "sqrt": sqrt_parts, "silu": silu_gate, "mix": mix_part_hi}[what](arg)
            nc.scalar.preload_act_table_set("natural_log_exp_and_others")

            def x1_squares(i):
                t, d = i % TT, i // TT
                act.wait_ge(x1_done, i + 1)
                if i >= 1:
                    act.wait_ge(x1sq_done, i)
                nc.scalar.activation(sq_sb, x1[:, t, d * CH:(d + 1) * CH], ACT.Square, accum_out=ssq[:, t, d:d + 1]).then_inc(x1sq_done, 1)

            for what, arg in steps_of(ACT_O):
                {"split": split_hi, "sq": x1_squares, "xT": x1T_hi,
                 "rms1": lambda _: inv_sqrt(ms1_done, 1, ms1, rstd1, y1_done)}[what](arg)

            def kqT_copy(kq):
                dst = (keyT, queryT)[kq % 2]
                for t in range(TT):
                    i = 2 * kq + t
                    act.wait_ge(t_done, i + 1)
                    nc.scalar.activation(dst[:, HG * (kq // 2):HG * (kq // 2 + 1), t * P:(t + 1) * P],
                                         heads(turn_bank("kqT", i)[:, :]), ACT.Copy).then_inc(tcopy_done, 1)

            def exps(h):
                act.wait_ge(nb_done, h + 1)
                if h >= 2:
                    act.wait_ge(pt_done, h - 1)
                sc = bank[6 + h % 2]
                nc.scalar.activation(prob[:, h % 2, 0:P], sc[:, 0:P], ACT.Exp, scale=q_scale[:, 0, h:h + 1],
                                     bias=nbias[:, 0, h:h + 1], accum_out=psum_l[:, h, 0:1])
                nc.scalar.activation(prob[:, h % 2, P:3 * P], sc[:, P:3 * P], ACT.Exp, scale=q_scale[:, 1, h:h + 1],
                                     bias=nbias[:, 1, h:h + 1], accum_out=psum_l[:, h, 1:2]).then_inc(p_done, 1)
                if h == H - 1:
                    nc.scalar.preload_act_table_set("silu_and_others")

            def oT_hi(i):
                t, g = i % TT, i // TT
                act.wait_ge(ot_done, i + 1)
                nc.scalar.activation(mix_hi[:, HG * g:HG * (g + 1), t * P:(t + 1) * P], heads(turn_bank("oT", i)[:, :]),
                                     ACT.Copy).then_inc(mhi_done, 1)

            def way_out(n):
                t, kind, acc = n % TT, KINDS[n // TT], bank[n % 3]
                act.wait_ge(u_done, n + 1)
                if kind in "kq":
                    m = earlier(n, "kq")
                    if n == 0:
                        act.wait_ge(rstd1_done, 1)
                    if t == 0 and m:
                        act.wait_ge(msk_done, m // 2)
                    for h in range(HG):
                        if m or h:
                            act.wait_ge(sq_done, HG * m + h)
                        nc.scalar.activation(sq_sb[:, 0:DH], acc[:, h * DH:(h + 1) * DH], ACT.Square, scale=rstd1[:, t:t + 1],
                                             accum_out=ssk[:, HG * t + h:HG * t + h + 1]).then_inc(sq_done, 1)
                elif kind == "v":
                    nc.scalar.activation(value[:, t, HALF[n // TT] * CH:(HALF[n // TT] + 1) * CH], acc[:, :], ACT.Copy,
                                         scale=rstd1[:, t:t + 1]).then_inc(v_done, 1)
                else:
                    m = earlier(n, "g")
                    if m == 0:
                        act.wait_ge(kq_done, 4)
                    if m >= 2:
                        act.wait_ge(og_done, m - 1)
                    nc.scalar.activation(gate[:, m % 2], acc[:, :], ACT.Silu, scale=rstd1[:, t:t + 1]).then_inc(gate_done, 1)

            def rms(kq):
                inv_sqrt(msk_done, kq + 1, msk, nyk, yk_done)

            for what, arg in steps_of(ACT_B):
                {"out": way_out, "split": split_hi, "rms": rms, "kqT": kqT_copy, "exp": exps, "oT": oT_hi}[what](arg)

        @block.vector
        def _(dve):
            steps = [0]

            def step(ins):
                steps[0] += 1
                ins.then_inc(dve_step, 1)
                dve.wait_ge(dve_step, steps[0])

            def split_lo(u):
                c, ks, cs = unit(u)
                dve.wait_ge(hi_done, u + 1)
                gamma = CHUNKS[c][1]
                if gamma is None:
                    last = nc.vector.tensor_tensor(w_lo[:, c % WR, ks, cs], raw_unit(u), w_hi[:, c % WR, ks, cs].bitcast(F32), ALU.subtract)
                else:
                    for k in range(UK):
                        last = nc.vector.scalar_tensor_tensor(w_lo[:, c % WR, ks.start + k, :], raw_unit(u)[:, k],
                                                              V(gamma)[:, ks.start + k:ks.start + k + 1],
                                                              w_hi[:, c % WR, ks.start + k, :].bitcast(F32), ALU.mult, ALU.subtract)
                last.then_inc(lo_done, 1)

            def refine(y, ms, t, out):
                step(nc.vector.tensor_tensor(t, y, y, ALU.mult))
                step(nc.vector.scalar_tensor_tensor(t, t, -0.5, ms, ALU.mult, ALU.mult))
                return nc.vector.scalar_tensor_tensor(out, t, 1.5, y, ALU.add, ALU.mult)

            dve.wait_ge(vec_in, 16)
            neg, mag, e, s_, s2, q = (lru[:, n, :] for n in (6, 4, 5, 0, 1, 7))
            step(nc.vector.tensor_scalar(neg, V("lambda"), -1.0, None, ALU.mult))
            nc.vector.tensor_tensor(mag, V("lambda"), neg, ALU.max).then_inc(lam_abs, 1)
            step(nc.vector.tensor_scalar(rb_half, V("r_b"), 0.5, None, ALU.mult))
            step(nc.vector.tensor_scalar(ib_half, V("i_b"), 0.5, None, ALU.mult))
            dve.wait_ge(lam_exp, 1)
            step(nc.vector.tensor_scalar(q, e, 2.0, None, ALU.add))
            step(nc.vector.reciprocal(s_, q))
            step(nc.vector.tensor_tensor(s_, e, s_, ALU.mult))
            step(nc.vector.tensor_tensor(s2, s_, s_, ALU.mult))
            step(nc.vector.tensor_scalar(q, s2, 1.0 / 15, None, ALU.mult))
            for n in range(UPC):
                dve.wait_ge(hhi_done, n + 1)
                for k in (2 * n, 2 * n + 1):
                    last = nc.vector.scalar_tensor_tensor(act_lo[:, k, :], xT_sb[:, k, :], V("a_norm")[:, k:k + 1],
                                                          act_hi[:, k, :].bitcast(F32), ALU.mult, ALU.subtract)
                last.then_inc(hlo_done, 1)
                for odd in ((13, 11), (9,), (7, 5), (3,))[n]:
                    step(nc.vector.scalar_tensor_tensor(q, q, 1.0 / odd, s2, ALU.add, ALU.mult))
                if n % 2 == 0:
                    split_lo(n // 2)
            dve.wait_ge(stat_done, 1)
            nc.vector.tensor_scalar(ms0, bank[6][:, 0:S], 1.0 / D, EPS, ALU.mult, ALU.add).then_inc(ms0_done, 1)
            split_lo(2)
            dve.wait_ge(y0_done, 2)
            refine(y0, ms0, t0, rstd0).then_inc(rstd0_done, 1)
            dve.wait_ge(rstd0_done, 1)

            def scale_x(b):
                dve.wait_ge(x_done, b + 1)
                nc.vector.tensor_tensor(xs[:, b, :], bank[b % 4][:, 0:S], rstd0, ALU.mult).then_inc(xs_done, 1)

            scale_x(0)
            split_lo(3)
            step(nc.vector.scalar_tensor_tensor(q, q, 1.0, s_, ALU.add, ALU.mult))
            step(nc.vector.tensor_scalar(neg, neg, 0.0, -RG_C / 2, ALU.max, ALU.mult))
            step(nc.vector.scalar_tensor_tensor(decay_half, q, -RG_C, neg, ALU.mult, ALU.add))
            nc.vector.tensor_scalar(decay_neg, decay_half, -0.5, None, ALU.mult).then_inc(lru_made, 1)

            def convolve(b):
                dve.wait_ge(tap0_done, b + 1)
                for back in (1, 2, 3):
                    if back > 1:
                        dve.wait_ge(conv_done, 3 * b + back - 1)
                    nc.vector.scalar_tensor_tensor(conv[:, b, back:S], xs[:, b, 0:S - back], V(f"conv_w{3 - back}")[:, b:b + 1],
                                                   conv[:, b, back:S], ALU.mult, ALU.add).then_inc(conv_done, 1)

            def recur(b):
                dve.wait_ge(b_done, b + 1)
                nc.vector.tensor_tensor_scan(state[:, b, :], decay[:, b, :], igate[:, b, :], 0.0, ALU.mult, ALU.add).then_inc(scan_done, 1)

            def gate_out(b):
                dve.wait_ge(g_done, b + 1)
                dve.wait_ge(ix_done, b + 1)
                nc.vector.tensor_tensor(zs[:, b, :], bank[b % 4][:, 0:S], rstd0, ALU.mult).then_inc(zs_done, 1)

            def gate_mix(b):
                dve.wait_ge(silu_done, b + 1)
                dve.wait_ge(scan_done, b + 1)
                nc.vector.tensor_tensor(mix[:, b, :], silu_z[:, b, :], state[:, b, :], ALU.mult).then_inc(mix_done, 1)

            def gated_x(b):
                dve.wait_ge(gates_done, 2 * b + 2)
                nc.vector.scalar_tensor_tensor(igate[:, b, :], igate[:, b, :], 1.0, conv[:, b, :], ALU.add, ALU.mult).then_inc(ix_done, 1)

            def one_plus_decay(b):
                dve.wait_ge(ix_done, b + 1)
                dve.wait_ge(decay_done, 2 * b + 1)
                nc.vector.scalar_tensor_tensor(igate[:, b, :], decay[:, b, :], 1.0, igate[:, b, :], ALU.add, ALU.mult).then_inc(ia_done, 1)

            def mix_part_lo(p):
                dve.wait_ge(mhi_done, p + 1)
                nc.vector.tensor_tensor(mix_lo[:, 2 * p:2 * p + 2, :], mix[:, 2 * p:2 * p + 2, :],
                                        mix_hi[:, 2 * p:2 * p + 2, :].bitcast(F32), ALU.subtract).then_inc(mlo_done, 1)

            for b in range(NB):
                if b:
                    scale_x(b)
                for u in SPLIT_X[b]:
                    split_lo(u)
                convolve(b)
                if b >= 3:
                    gated_x(b - 3)
            for what, arg in steps_of(DVE_G):
                {"split": split_lo, "ix": gated_x, "ia": one_plus_decay, "zs": gate_out, "scan": recur, "mix": gate_mix,
                 "lo": mix_part_lo}[what](arg)

            def x1T_lo(i):
                t, d = i % TT, i // TT
                dve.wait_ge(xhi_done, i + 1)
                nc.vector.tensor_tensor(act_lo[:, 4 * d:4 * d + 4, t * P:(t + 1) * P], heads(turn_bank("x1T", i)[:, :]),
                                        act_hi[:, 4 * d:4 * d + 4, t * P:(t + 1) * P].bitcast(F32), ALU.subtract).then_inc(xlo_done, 1)

            def add_x1(i):
                t, d = i % TT, i // TT
                dve.wait_ge(o_done, i + 1)
                if i == 0:
                    dve.wait_ge(scan_done, NB)
                    dve.wait_ge(x_in, 16)
                nc.vector.tensor_tensor(x1[:, t, d * CH:(d + 1) * CH], bank[O_BANKS[i]][:, :], x_sb[:, t, d * CH:(d + 1) * CH],
                                        ALU.add).then_inc(x1_done, 1)

            def x1_rms(_):
                dve.wait_ge(x1sq_done, 4)
                step(nc.vector.tensor_tensor(ms1, ssq[:, :, 0], ssq[:, :, 1], ALU.add))
                nc.vector.tensor_scalar(ms1, ms1, 1.0 / D, EPS, ALU.mult, ALU.add).then_inc(ms1_done, 1)
                dve.wait_ge(ms1_done, 1)
                dve.wait_ge(y1_done, 2)
                refine(rstd1, ms1, nt1, rstd1).then_inc(rstd1_done, 1)

            for what, arg in steps_of(DVE_O):
                {"split": split_lo, "x1": add_x1, "xT": x1T_lo, "rms1": x1_rms}[what](arg)

            def norm_rope(kq):
                slot = roped[kq % 2]
                dve.wait_ge(msk_done, kq + 1)
                dve.wait_ge(yk_done, 2 * kq + 2)
                step(refine(nyk, msk, ntk, nyk))
                y3 = nyk.rearrange("p (t h) -> p t h", t=TT)
                n3 = ntk.rearrange("p (t h) -> p t h", t=TT)
                r1 = rstd1.unsqueeze(2).to_broadcast([P, TT, HG])
                dve.wait_ge(add_done, 2 * kq + 2)
                if kq % 2 == 0:
                    step(nc.vector.tensor_tensor(n3, y3, r1, ALU.mult))
                    for t in range(TT):
                        last = nc.vector.tensor_tensor(heads(slot[:, t]), heads(slot[:, t]),
                                                       n3[:, t].unsqueeze(2).to_broadcast([P, HG, DH]), ALU.mult)
                    last.then_inc(kq_done, 1)
                else:
                    g = kq // 2
                    step(nc.vector.scalar_tensor_tensor(q_scale[:, :, HG * g:HG * (g + 1)], y3, SCALE, r1, ALU.mult, ALU.mult))
                    nc.vector.tensor_scalar(q_nscale[:, :, HG * g:HG * (g + 1)], q_scale[:, :, HG * g:HG * (g + 1)], -1.0, None,
                                            ALU.mult).then_inc(kq_done, 1)

            def mean_square(kq):
                dve.wait_ge(sq_done, 2 * HG * (kq + 1))
                nc.vector.tensor_scalar(msk, ssk, 1.0 / DH, EPS, ALU.mult, ALU.add).then_inc(msk_done, 1)

            def maxima(h):
                sc = bank[6 + h % 2]
                dve.wait_ge(s_done, h + 1)
                nc.vector.reduce_max(smax[:, 0, h:h + 1], sc[:, 0:P], AX_X)
                step(nc.vector.reduce_max(smax[:, 1, h:h + 1], sc[:, P:3 * P], AX_X))
                nc.vector.tensor_tensor(nbias[:, :, h], smax[:, :, h], q_nscale[:, :, h], ALU.mult).then_inc(nb_done, 1)

            def probT_copy(h):
                dve.wait_ge(pt_done, h + 1)
                if h >= 2:
                    dve.wait_ge(pv_done, h - 1)
                nc.vector.tensor_copy(probT[:, h % 2], turn_bank("pT", h)[:, 0:3 * P]).then_inc(ptc_done, 1)

            def attend(u):
                g, h0 = 2 * u // HG, 2 * u % HG
                dve.wait_ge(pv_done, 2 * u + 2)
                step(nc.vector.reciprocal(recip_l[:, 2 * u:2 * u + 2, :], psum_l[:, 2 * u:2 * u + 2, :]))
                for hh in range(2):
                    last = nc.vector.tensor_tensor(att[g][:, :, (h0 + hh) * DH:(h0 + hh + 1) * DH],
                                                   bank[3][:, hh * 2 * P:(hh + 1) * 2 * P].rearrange("p (t d) -> p t d", t=TT),
                                                   recip_l[:, 2 * u + hh, :].unsqueeze(2).to_broadcast([P, TT, DH]), ALU.mult)
                last.then_inc(on_done, 1)

            def oT_lo(i):
                t, g = i % TT, i // TT
                dve.wait_ge(mhi_done, NB // 2 + i + 1)
                nc.vector.tensor_tensor(mix_lo[:, HG * g:HG * (g + 1), t * P:(t + 1) * P], heads(turn_bank("oT", i)[:, :]),
                                        mix_hi[:, HG * g:HG * (g + 1), t * P:(t + 1) * P].bitcast(F32), ALU.subtract).then_inc(mlo_done, 1)

            def way_out(n):
                t, kind, acc = n % TT, KINDS[n // TT], bank[n % 3]
                if kind in "kq":
                    m = earlier(n, "kq")
                    kq = m // 2
                    slot = roped[kq % 2]
                    table = 2 * (kq % 2)
                    half = DH // 2
                    if m == 0:
                        dve.wait_ge(table_made, 4)
                    else:
                        dve.wait_ge(add_done, m)
                    dve.wait_ge(sq_done, HG * (m + 1))
                    if kq >= 2:
                        dve.wait_ge(t_done, 2 * (kq - 1))
                    nc.vector.tensor_tensor(heads(slot[:, t]), heads(acc[:, :]),
                                            rope_t[:, table, t].unsqueeze(1).to_broadcast([P, HG, DH]), ALU.mult)
                    for to, fro in ((0, half), (half, 0)):
                        last = nc.vector.tensor_tensor(heads(swap_sb)[:, :, to:to + half], heads(acc[:, :])[:, :, fro:fro + half],
                                                       rope_t[:, table + 1, t, to:to + half].unsqueeze(1).to_broadcast([P, HG, half]), ALU.mult)
                    last.then_inc(cos_done, 1)
                    dve.wait_ge(cos_done, m + 1)
                    nc.vector.tensor_tensor(slot[:, t], slot[:, t], swap_sb, ALU.add).then_inc(add_done, 1)

            def gate_attention(m):
                t, g = m % TT, m // TT
                dve.wait_ge(gate_done, m + 1)
                dve.wait_ge(on_done, 2 * (g + 1))
                nc.vector.tensor_tensor(att[g][:, t], gate[:, m % 2], att[g][:, t], ALU.mult).then_inc(og_done, 1)

            for what, arg in steps_of(DVE_B):
                {"out": way_out, "split": split_lo, "ms": mean_square, "norm": norm_rope, "max": maxima,
                 "probT": probT_copy, "attend": attend, "gate": gate_attention, "oT": oT_lo}[what](arg)

            for n, (i, c0, c1) in enumerate(Y_PARTS):
                t, d = i % TT, i // TT
                dve.wait_ge(f_done, n + 1)
                nc.vector.tensor_tensor(y_sb[:, i, c0:c1], y_bank(i, c0)[:, c0:c1], x1[:, t, d * CH + c0:d * CH + c1],
                                        ALU.add).then_inc(y_done, 1)

        @block.tensor
        def _(pe):
            def product(out, a_hi, a_lo, w, start, stop):
                nc.tensor.matmul(out, a_hi, w[0], start=start, stop=False)
                nc.tensor.matmul(out, a_hi, w[1], start=False, stop=False)
                return nc.tensor.matmul(out, a_lo, w[0], start=False, stop=stop)

            def weights_ready(c, k):
                if k % UK == 0:
                    pe.wait_ge(lo_done, UPC * c + k // UK + 1)

            pe.wait_ge(const_made, 1)
            for _ in range(WARM):
                nc.tensor.matmul(bank[7][:, 0:P], ones[:, :], ones[:, :], start=True, stop=True)
            def channels(c, b, done, first, gates_at):
                cols_ = slice((b % 4) * P, (b % 4 + 1) * P)
                out = bank[b % 4][:, 0:S]
                for k in range(KT):
                    if k in gates_at:
                        gate_products(gates_at[k])
                    if first and k % UK == 0:
                        for n in {0: (0, 1), UK: (2,), 2 * UK: (3,)}.get(k, ()):
                            pe.wait_ge(squared, n + 1)
                            for j in range(n * UK, (n + 1) * UK):
                                last = nc.tensor.matmul(bank[6][:, 0:S], ones[:, :], square[:, j, :], start=(j == 0), stop=(j == KT - 1))
                            if j == KT - 1:
                                last.then_inc(stat_done, 1)
                        pe.wait_ge(hlo_done, k // UK + 1)
                    if c == 0:
                        if b % 2 == 0 and k % (2 * UK) == 0:
                            pe.wait_ge(lo_done, b + k // (2 * UK) + 1)
                    elif b % 4 == 0:
                        weights_ready(c, k)
                    wh, wl = w_hi[:, c % WR, k, cols_], w_lo[:, c % WR, k, cols_]
                    nc.tensor.matmul(out, wh, act_hi[:, k, :], start=(k == 0), stop=False)
                    nc.tensor.matmul(out, wh, act_lo[:, k, :], start=False, stop=False)
                    last = nc.tensor.matmul(out, wl, act_hi[:, k, :], start=False, stop=(k == KT - 1))
                last.then_inc(done, 1)

            def gate_products(b):
                pri = bank[4 + b % 2]
                pe.wait_ge(conv_done, 3 * b + 3)
                if b == 0:
                    pe.wait_ge(gate_w_in, 32)
                if b >= 2:
                    pe.wait_ge(gates_done, 2 * (b - 1))
                nc.tensor.matmul(pri[:, 0:S], rw[:, b, :], conv[:, b, :], start=True, stop=True)
                nc.tensor.matmul(pri[:, S:2 * S], iw[:, b, :], conv[:, b, :], start=True, stop=True).then_inc(ri_done, 1)

            for b in range(NB):
                if b >= 4:
                    pe.wait_ge(xs_done, b - 3)
                channels(b // 4, b, x_done, b == 0, GATES_AT.get(b, {}))
            for b in range(NB):
                if b < 4:
                    pe.wait_ge(xs_done, b + 5)
                else:
                    pe.wait_ge(zs_done, b - 3)
                channels(2 + b // 4, b, g_done, False, GATES_AT.get(NB + b, {}))

            def x1_turn(i):
                t, d = i % TT, i // TT
                out = turn_bank("x1T", i)
                pe.wait_ge(x1_done, i + 1)
                pe.wait_ge(*turn_free("x1T", i))
                if i == 0:
                    pe.wait_ge(ident_in, 16)
                for k in range(4):
                    last = nc.tensor.transpose(out[:, k * P:(k + 1) * P], x1[:, t, d * CH + k * P:d * CH + (k + 1) * P], ident[:, :])
                last.then_inc(xt_done, 1)

            for i, k0, k1 in ((0, 0, 4), (1, 0, 4), (0, 4, 6), (1, 4, 6), (0, 6, 8), (1, 6, 8), (2, 0, 8), (3, 0, 8)):
                t, d = i % TT, i // TT
                c = C_OUT_A + d
                if k0 == 0 and i >= 2:
                    pe.wait_ge(zs_done, 4 + O_BANKS[i] + 1)
                for k in range(k0, k1):
                    if (i, k) in X1_TURN_AT:
                        x1_turn(X1_TURN_AT[i, k])
                    if t == 0:
                        weights_ready(c, k)
                    if i == 0 and k % 2 == 0:
                        pe.wait_ge(mlo_done, k // 2 + 1)
                    last = product(bank[O_BANKS[i]][:, :], mix_hi[:, k, t * P:(t + 1) * P], mix_lo[:, k, t * P:(t + 1) * P],
                                   (w_hi[:, c % WR, k, :], w_lo[:, c % WR, k, :]), k == 0, k == KT - 1)
                if k1 == KT:
                    last.then_inc(o_done, 1)

            def kq_turn(kq):
                slot = roped[kq % 2]
                pe.wait_ge(kq_done, kq + 1)
                for t in range(TT):
                    i = 2 * kq + t
                    pe.wait_ge(*turn_free("kqT", i))
                    for h in range(HG):
                        last = nc.tensor.transpose(turn_bank("kqT", i)[:, h * P:(h + 1) * P], slot[:, t, h * DH:(h + 1) * DH], ident[:, :])
                    last.then_inc(t_done, 1)

            def scores(h):
                sc = bank[6 + h % 2]
                pe.wait_ge(tcopy_done, 4 * (h // HG + 1))
                if h == 0:
                    pe.wait_ge(const_made, 3)
                if h >= 2:
                    pe.wait_ge(p_done, h - 1)
                nc.tensor.matmul(sc[:, 0:P], queryT[:, h, 0:P], keyT[:, h, 0:P], start=True, stop=False)
                nc.tensor.matmul(sc[:, 0:P], ident_b[:, :], mask_b[:, :], start=False, stop=True)
                nc.tensor.matmul(sc[:, P:3 * P], queryT[:, h, P:2 * P], keyT[:, h, 0:2 * P], start=True, stop=False)
                nc.tensor.matmul(sc[:, 2 * P:3 * P], ident_b[:, :], mask_b[:, :], start=False, stop=True).then_inc(s_done, 1)

            def prob_turn(h):
                pe.wait_ge(p_done, h + 1)
                pe.wait_ge(*turn_free("pT", h))
                for i in range(3):
                    last = nc.tensor.transpose(turn_bank("pT", h)[:, i * P:(i + 1) * P], prob[:, h % 2, i * P:(i + 1) * P], ident[:, :])
                last.then_inc(pt_done, 1)

            def weighted_values(h):
                pe.wait_ge(ptc_done, h + 1)
                pe.wait_ge(v_done, 2 * (h // HG + 1))
                if h == 0:
                    pe.wait_ge(x1_done, 4)
                elif h % 2 == 0:
                    pe.wait_ge(on_done, h // 2)
                at = (h % 2) * 2 * P
                pT = probT[:, h % 2]
                v = [value[:, t, h * DH:(h + 1) * DH] for t in range(TT)]
                nc.tensor.matmul(bank[3][:, at:at + P], pT[:, 0:P], v[0], start=True, stop=True)
                nc.tensor.matmul(bank[3][:, at + P:at + 2 * P], pT[:, P:2 * P], v[0], start=True, stop=False)
                nc.tensor.matmul(bank[3][:, at + P:at + 2 * P], pT[:, 2 * P:3 * P], v[1], start=False, stop=True).then_inc(pv_done, 1)

            def mix_turn(i):
                t, g = i % TT, i // TT
                pe.wait_ge(og_done, i + 1)
                pe.wait_ge(*turn_free("oT", i))
                for h in range(HG):
                    last = nc.tensor.transpose(turn_bank("oT", i)[:, h * P:(h + 1) * P], att[g][:, t, h * DH:(h + 1) * DH], ident[:, :])
                last.then_inc(ot_done, 1)

            small = {"kqT": kq_turn, "scores": scores, "pT": prob_turn, "pv": weighted_values, "oT": mix_turn}

            def beside(n, k):
                for text in PE_B.get((n, k), []):
                    name, arg = text.split()
                    small[name](int(arg))

            for n, k0, k1 in [(0, 0, 4), (1, 0, 4), (0, 4, 8), (1, 4, 8)] + [(n, 0, KT) for n in range(2, 16)]:
                t, c = n % TT, C_B + n // TT
                if k0 == 0:
                    pe.wait_ge(*acc_free(n))
                for k in range(k0, k1):
                    if (n, k) == (0, 3):
                        x1_turn(3)
                    beside(n, k)
                    if t == 0:
                        weights_ready(c, k)
                    if n < 2 and k % 4 == 0:
                        pe.wait_ge(xlo_done, 2 * (k // 4) + t + 1)
                    last = product(bank[n % 3][:, :], act_hi[:, k, t * P:(t + 1) * P], act_lo[:, k, t * P:(t + 1) * P],
                                   (w_hi[:, c % WR, k, :], w_lo[:, c % WR, k, :]), k == 0, k == KT - 1)
                if k1 == KT:
                    last.then_inc(u_done, 1)

            for i, c0, c1 in Y_PARTS:
                t, d = i % TT, i // TT
                c = C_OUT_B + d
                if i < 3:
                    pe.wait_ge(*acc_free(16 + i))
                elif c0 == 0:
                    pe.wait_ge(y_done, 1)
                else:
                    pe.wait_ge(y_done, 2)
                for k in range(KT):
                    if c0 == 0:
                        beside(16 + i, k)
                    if t == 0:
                        weights_ready(c, k)
                    if i < 2 and k % 4 == 0:
                        pe.wait_ge(mlo_done, NB // 2 + 2 * (k // 4) + t + 1)
                    last = product(y_bank(i, c0)[:, c0:c1], mix_hi[:, k, t * P:(t + 1) * P], mix_lo[:, k, t * P:(t + 1) * P],
                                   (w_hi[:, c % WR, k, c0:c1], w_lo[:, c % WR, k, c0:c1]), k == 0, k == KT - 1)
                last.then_inc(f_done, 1)

    return nc


def kernel(**inputs):
    import numpy as np
    import concourse.bacc as bacc
    from concourse.bass_utils import run_bass_kernel_spmd

    a = {n: np.asarray(v) for n, v in inputs.items()}
    x = a["x"][0]
    S, D = x.shape
    DH = a["k_norm"].shape[0]
    half = DH // 2
    named = {"conv_b": a["a_conv_b"][0], "r_b": a["a_r_b"][0], "i_b": a["a_i_b"][0], "lambda": a["a_lambda"][0],
             "a_norm": a["a_norm"][0], "kv_norm": a["kv_norm"], "b_norm": a["b_norm"][0]}
    named.update({f"conv_w{k}": a["a_conv_w"][0, k] for k in range(4)})
    inv = np.float32(10000.0) ** (-np.arange(half, dtype=np.float32) / np.float32(half))
    angle = np.arange(S, dtype=np.float32)[:, None] * inv[None, :].astype(np.float32)
    cos, sin = np.cos(angle), np.sin(angle)
    table = np.stack([np.concatenate([cos, cos], 1), np.concatenate([-sin, sin], 1)]).astype(np.float32)
    arrays = {
        "xT": x.T, "x_rows": x, "in_w": a["a_in_w"][0], "r_w": a["a_r_w"][0], "i_w": a["a_i_w"][0],
        "a_out_w": a["a_out_w"][0], "kv_w": a["kv_w"], "b_in_w": a["b_in_w"][0], "b_out_w": a["b_out_w"][0],
        "vectors": np.stack([named[n].reshape(D // P, P).T for n in VECTORS], 1),
        "head_norms": np.stack([a["k_norm"], a["q_norm"][0]]),
        "rope_cs": table.reshape(2, S // P, P, DH).transpose(0, 2, 1, 3),
        "ident_in": np.eye(P, dtype=np.float32),
    }
    arrays = {n: np.ascontiguousarray(v) for n, v in arrays.items()}
    nc = bacc.Bacc("TRN2", target_bir_lowering=False, num_devices=1)
    args = [nc.dram_tensor(n, v.shape, mybir.dt.from_np(v.dtype), kind="ExternalInput").ap() for n, v in arrays.items()]
    y = nc.dram_tensor("y", (S, D), F32, kind="ExternalOutput").ap()
    hybrid_trunk(nc, *args, y)
    r = run_bass_kernel_spmd(nc, [arrays], core_ids=[0])
    return r.results[0]["y"].reshape(1, S, D)
```

```python
from contextlib import ExitStack

import concourse.bass as bass
from concourse import mybir

P = 128
F32 = mybir.dt.float32
F32R = mybir.dt.float32r
BF16 = mybir.dt.bfloat16
ALU = mybir.AluOpType
ACT = mybir.ActivationFunctionType
AX_X = mybir.AxisListType.X
EPS = 1e-6
NEG_INF = -1e30
RG_C = 8.0

VECTORS = ["conv_w0", "conv_w1", "conv_w2", "conv_w3", "conv_b", "r_b", "i_b", "lambda", "a_norm", "kv_norm", "b_norm"]


def hybrid_trunk(nc, xT, x, in_w, r_w, i_w, a_out_w, kv_w, b_in_w, b_out_w, vectors, head_norms, rope_cs, identity, y):
    D, S = xT.shape
    KT = D // P
    TT = S // P
    NB = r_w.shape[0]
    CH = 512
    UK = 2
    UPC = KT // UK
    DH = P
    H = D // DH
    HG = CH // DH
    SCALE = float(DH) ** -0.5
    assert D == 1024 and S == 256 and NB == KT and in_w.shape[1] == 2 * D

    def cols(w, c):
        return w[:, c * CH:(c + 1) * CH]

    CHUNKS = [(cols(in_w, c), None) for c in range(4)]
    CHUNKS += [(cols(a_out_w, c), None) for c in range(2)]
    CHUNKS += [(cols(kv_w, 0), "kv_norm"), (cols(b_in_w, 0), "b_norm"), (cols(kv_w, 2), "kv_norm")]
    CHUNKS += [(cols(kv_w, 1), "kv_norm"), (cols(b_in_w, 1), "b_norm"), (cols(kv_w, 3), "kv_norm")]
    CHUNKS += [(cols(b_in_w, 2), "b_norm"), (cols(b_in_w, 3), "b_norm")]
    CHUNKS += [(cols(b_out_w, c), None) for c in range(2)]
    KINDS = ["k", "q", "v", "k", "q", "v", "g", "g"]
    HALF = [0, 0, 0, 1, 1, 1, 0, 1]
    C_OUT_A, C_B, C_OUT_B = 4, 6, 14
    NU = len(CHUNKS) * UPC
    Y_PARTS = [(0, 0, CH), (1, 0, CH), (2, 0, CH), (3, 0, CH // 2), (3, CH // 2, CH)]
    GATES_AT = {3: {1: 0}, 4: {6: 1}, 5: {0: 2}, 6: {2: 3}, 7: {2: 4}, 8: {0: 5, 6: 6}, 9: {3: 7}}
    X1_TURN_AT = {(2, 1): 0, (2, 2): 1, (3, 4): 2}
    WARM = 10
    RAW = 4
    WR = 3

    def unit(u):
        c, n = u // UPC, u % UPC
        if c == 0:
            k0, c0 = n % 2 * 2 * UK, n // 2 * (CH // 2)
            return c, slice(k0, k0 + 2 * UK), slice(c0, c0 + CH // 2)
        return c, slice(n * UK, (n + 1) * UK), slice(0, CH)

    ACT_G = ("tap:0 4 tap:1 5 6 tap:2 7 gates:0 tap:3 8 gates:1 tap:4 gates:2 9 tap:5 gates:3 10 tap:6 gates:4 11 "
             "12 tap:7 gates:5 13 gates:6 gates:7 14 15 16 sqrt silu:0 silu:1 silu:2 17 silu:3 silu:4 mix:0 18 19 "
             "silu:5 mix:1 silu:6 mix:2 silu:7 20 mix:3")
    DVE_G = ("conv:0 conv:1 xs:1 conv:2 4 conv:3 conv:4 xs:2 conv:5 5 6 conv:6 xs:3 conv:7 7 conv:8 conv:9 ix:0 "
             "conv:10 xs:4 conv:11 8 conv:12 ix:1 conv:13 xs:5 conv:14 9 conv:15 conv:16 xs:6 conv:17 10 conv:18 "
             "ix:2 ix:3 conv:19 xs:7 conv:20 11 conv:21 ix:4 conv:22 conv:23 12 13 ia:0 ix:5 ix:6 ix:7 zs:0 ia:1 "
             "ia:2 zs:1 ia:3 ia:4 ia:5 ia:6 14 15 zs:2 16 zs:3 scan:0 scan:1 ia:7 scan:2 scan:3 mix:0 mix:1 zs:4 "
             "scan:4 17 mix:2 mix:3 scan:5 18 zs:5 lo:0 scan:6 scan:7 lo:1 mix:4 19 zs:6 mix:5 zs:7 mix:6 mix:7 "
             "lo:2 20 lo:3")
    ACT_O = "21 22 23 sq:0 xT:0 xT:1 24 sq:1 25 26 27 sq:2 28 xT:2 29 sq:3 30 xT:3 rms1"
    DVE_O = "21 22 23 x1:0 x1:1 xT:0 xT:1 24 25 x1:2 26 27 28 xT:2 x1:3 29 30 xT:3 rms1"
    PE_B = {(3, 7): ["kqT 0"], (5, 4): ["kqT 1"], (5, 7): ["scores 0", "scores 1"], (6, 2): ["pT 0"],
            (6, 5): ["scores 2", "pT 1"], (6, 7): ["pv 0"], (7, 2): ["scores 3"], (7, 7): ["pv 1"],
            (8, 0): ["pT 2"], (8, 4): ["pT 3"], (8, 6): ["pv 2"], (9, 0): ["pv 3"], (9, 4): ["kqT 2"],
            (11, 1): ["kqT 3"], (11, 4): ["scores 4", "scores 5"], (12, 3): ["pT 4"],
            (12, 4): ["scores 6", "pT 5"], (13, 0): ["pv 4", "scores 7", "pT 6"], (13, 3): ["pv 5", "pT 7"],
            (13, 6): ["pv 6"], (14, 3): ["pv 7", "oT 0"], (14, 6): ["oT 1"], (16, 0): ["oT 2"],
            (16, 5): ["oT 3"]}
    ACT_B = ("31 out:0 32 33 34 out:1 rms:0 out:2 35 36 out:3 37 rms:1 kqT:0 38 39 40 out:4 kqT:1 exp:0 out:5 exp:1 "
             "41 42 out:6 exp:2 43 exp:3 44 out:7 rms:2 out:8 45 46 47 out:9 kqT:2 rms:3 48 49 kqT:3 50 exp:4 "
             "out:10 out:11 exp:5 51 52 exp:6 exp:7 out:12 53 54 out:13 55 oT:0 56 57 oT:1 out:14 58 59 60 oT:2 61 "
             "out:15 oT:3 62 63")
    DVE_B = ("31 out:0 32 33 34 ms:0 out:1 norm:0 out:2 35 36 ms:1 out:3 norm:1 37 38 39 40 max:0 max:1 41 probT:0 "
             "max:2 42 probT:1 max:3 43 out:6 probT:2 ms:2 attend:0 out:7 probT:3 44 norm:2 attend:1 45 out:8 46 47 "
             "ms:3 out:9 norm:3 48 49 50 max:4 max:5 51 probT:4 max:6 probT:5 52 max:7 probT:6 attend:2 53 54 "
             "probT:7 gate:0 55 gate:1 56 attend:3 oT:0 57 gate:2 oT:1 58 59 oT:2 gate:3 60 oT:3 61 62 63")

    def steps_of(text):
        for word in text.split():
            name, _, arg = word.partition(":")
            yield ("split", int(name)) if name.isdecimal() else (name, int(arg) if arg else None)

    with ExitStack() as ctx:
        def sb(name, shape, dt=F32):
            return ctx.enter_context(nc.sbuf_tensor(name, shape, dt))

        def sem(name):
            return ctx.enter_context(nc.semaphore(name))

        raw = sb("raw", [P, RAW, UK * CH])
        w_hi = sb("w_hi", [P, WR, KT, CH], F32R)
        w_lo = sb("w_lo", [P, WR, KT, CH], F32R)
        act_hi = sb("act_hi", [P, KT, S], F32R)
        act_lo = sb("act_lo", [P, KT, S], F32R)
        mix_hi = sb("mix_hi", [P, KT, S], F32R)
        mix_lo = sb("mix_lo", [P, KT, S], F32R)
        buf = [sb(f"buf{n}", [P, KT * S]) for n in range(5)]
        scratch = sb("scratch", [P, 2560])
        rope_t = sb("rope_t", [P, 4, TT, DH])
        ident = sb("ident", [P, P])
        ident_b = sb("ident_b", [P, P], BF16)
        mask_b = sb("mask_b", [P, P], BF16)
        ones = sb("ones", [P, P])
        head_norm = sb("head_norm", [P, 2, DH])
        rope_b = sb("rope_b", [P, TT * CH])
        vec = sb("vec", [P, len(VECTORS), KT])
        lru = sb("lru", [P, 10, KT])
        small = sb("small", [P, 160])

        def ch3(t):
            return t[:, :].rearrange("p (k s) -> p k s", k=KT)

        def tok3(t):
            return t[:, :].rearrange("p (t c) -> p t c", t=TT)

        xT_sb, decay = ch3(buf[0]), ch3(buf[0])
        conv, zs, mix = ch3(buf[1]), ch3(buf[1]), ch3(buf[1])
        rgate, state = ch3(buf[2]), ch3(buf[2])
        xs, igate, silu_z = ch3(buf[3]), ch3(buf[3]), ch3(buf[3])
        square, drive = ch3(buf[4]), ch3(buf[4])
        ms0, y0, nt0, rstd0 = (rope_b[:, n * S:(n + 1) * S] for n in range(4))
        rw = scratch[:, 0:NB * P].rearrange("p (n j) -> p n j", n=NB)
        iw = scratch[:, NB * P:2 * NB * P].rearrange("p (n j) -> p n j", n=NB)
        x1 = tok3(buf[0])
        roped = [tok3(buf[1])[:, 0], rope_b[:, :]]
        roped = [r.rearrange("p (t c) -> p t c", t=TT) for r in roped]
        att = [tok3(buf[1])[:, 1], tok3(buf[1])[:, 0]]
        att = [r.rearrange("p (t c) -> p t c", t=TT) for r in att]
        value = tok3(buf[2])
        y_sb = buf[2][:, :].rearrange("p (i c) -> p i c", c=CH)
        keyT = ch3(buf[3])
        x_sb, queryT = tok3(buf[4]), ch3(buf[4])
        sq_sb = scratch[:, 0:CH]
        swap_sb = scratch[:, CH:2 * CH]
        gate = scratch[:, 0:2 * CH].rearrange("p (r c) -> p r c", r=2)
        prob = scratch[:, 1024:1024 + 768].rearrange("p (r c) -> p r c", r=2)
        probT = scratch[:, 1792:1792 + 768].rearrange("p (r c) -> p r c", r=2)

        def raw_unit(u):
            _, ks, cs = unit(u)
            return raw[:, u % RAW].rearrange("p (k c) -> p k c", c=cs.stop - cs.start)

        def V(name):
            return vec[:, VECTORS.index(name), :]

        decay_half, decay_neg, rb_half, ib_half = lru[:, 0, :], lru[:, 1, :], lru[:, 2, :], lru[:, 3, :]
        neg, mag, e, s_, s2, series = (lru[:, n, :] for n in (6, 4, 5, 8, 9, 7))
        ssq = small[:, 0:4].rearrange("p (t d) -> p t d", t=TT)
        ms1, rstd1, nt1 = (small[:, 4 + 2 * n:6 + 2 * n] for n in range(3))
        ssk = small[:, 12:20]
        msk, nyk, ntk = small[:, 20:28], small[:, 28:36], small[:, 36:44]
        q_scale = small[:, 44:60].rearrange("p (t h) -> p t h", t=TT)
        q_nscale = small[:, 60:76].rearrange("p (t h) -> p t h", t=TT)
        smax = small[:, 76:92].rearrange("p (t h) -> p t h", t=TT)
        nbias = small[:, 92:108].rearrange("p (t h) -> p t h", t=TT)
        psum_l = small[:, 108:124].rearrange("p (h t) -> p h t", t=TT)
        recip_l = small[:, 124:140].rearrange("p (h t) -> p h t", t=TT)

        bank = [ctx.enter_context(nc.psum_tensor(f"bank{n}", [P, 512], F32)) for n in range(8)]

        xT_in = [sem(f"xT_in{n}") for n in range(UPC)]
        x_in, vec_in, gate_w_in, table_in, ident_in = (sem(n) for n in ("x_in", "vec_in", "gate_w_in", "table_in", "ident_in"))
        raw_in = [sem(f"raw_in{n}") for n in range(RAW)]
        out_done = sem("out_done")
        hi_done, lo_done = sem("hi_done"), sem("lo_done")
        const_made, lru_made, table_made = sem("const_made"), sem("lru_made"), sem("table_made")
        pool_step = sem("pool_step")
        lam_exp, lam_abs, atanh_ready = sem("lam_exp"), sem("lam_abs"), sem("atanh_ready")
        squared, stat_done, ms0_done = sem("squared"), sem("stat_done"), sem("ms0_done")
        y0_done, rstd0_done = sem("y0_done"), sem("rstd0_done")
        hhi_done, hlo_done = sem("x_hi_done"), sem("x_lo_done")
        xs_done, zs_done = sem("xs_done"), sem("zs_done")
        x_done, ri_done, g_done = sem("x_done"), sem("ri_done"), sem("g_done")
        tap0_done, conv_done = sem("tap0_done"), sem("conv_done")
        gates_done, decay_done = sem("gates_done"), sem("decay_done")
        ix_done, ia_done, m_done = sem("ix_done"), sem("ia_done"), sem("m_done")
        b_done, scan_done, silu_done, mix_done = (sem(n) for n in ("b_done", "scan_done", "silu_done", "mix_done"))
        mhi_done, mlo_done = sem("mix_hi_done"), sem("mix_lo_done")
        o_done, x1_done, x1sq_done = sem("out_a_done"), sem("x1_done"), sem("x1sq_done")
        xt_done, xhi_done, xlo_done = sem("x1T_done"), sem("x1T_hi"), sem("x1T_lo")
        ms1_done, y1_done, rstd1_done = sem("ms1_done"), sem("y1_done"), sem("rstd1_done")
        u_done = sem("u_done")
        sq_done, cos_done, kq_done = sem("sq_done"), sem("cos_done"), sem("kq_done")
        msk_done, yk_done = sem("msk_done"), sem("yk_done")
        t_done, tcopy_done, v_done = sem("kqT_done"), sem("kqT_copied"), sem("v_done")
        s_done, nb_done, p_done, pt_done, ptc_done = (sem(n) for n in ("s_done", "nb_done", "p_done", "pt_done", "pt_copied"))
        pv_done, on_done = sem("pv_done"), sem("on_done")
        gate_done, og_done, ot_done = sem("gate_done"), sem("og_done"), sem("ot_done")
        f_done, y_done = sem("f_done"), sem("y_done")
        add_done = sem("add_done")
        dve_step = sem("dve_step")

        def earlier(n, kinds):
            return sum(KINDS[j // TT] in kinds for j in range(n))

        O_BANKS = [6, 7, 3, 2]

        def acc_free(n):
            if n < 2:
                return zs_done, 4 + n + 1
            if n == 2:
                return x1_done, 4
            m = n - 3
            kind = KINDS[m // 2]
            if kind in "kq":
                return cos_done, earlier(m + 1, "kq")
            return (v_done if kind == "v" else gate_done), earlier(m + 1, kind)

        def y_bank(i, c0):
            return bank[(16 + i + (c0 > 0)) % 3]

        TURNS = [("x1T", i, xlo_done, i + 1) for i in range(4)]
        TURNS += [("kqT", i, tcopy_done, i + 1) for i in range(4)]
        TURNS += [("pT", h, ptc_done, h + 1) for h in range(4)]
        TURNS += [("kqT", i, tcopy_done, i + 1) for i in range(4, 8)]
        TURNS += [("pT", h, ptc_done, h + 1) for h in range(4, 8)]
        TURNS += [("oT", i, mlo_done, NB // 2 + i + 1) for i in range(4)]
        TURN = {(what, i): n for n, (what, i, _, _) in enumerate(TURNS)}

        def turn_bank(what, i):
            return bank[4 + TURN[(what, i)] % 2]

        def turn_free(what, i):
            n = TURN[(what, i)]
            if n < 2:
                return gates_done, 2 * NB
            return TURNS[n - 2][2], TURNS[n - 2][3]

        block = ctx.enter_context(nc.Block())

        @block.sync
        def _(sp):
            def load(u):
                if u >= RAW:
                    sp.wait_ge(lo_done, u - RAW + 1)
                c, ks, cs = unit(u)
                w = CHUNKS[c][0][ks.start * P:ks.stop * P, cs].rearrange("(k p) c -> p k c", p=P)
                sp.dma_start(raw_unit(u), w).then_inc(raw_in[u % RAW], 16)

            sp.dma_start(vec[:, :, :], vectors).then_inc(vec_in, 16)
            xT_v = xT.rearrange("(k p) s -> p k s", p=P)
            for n in range(UPC):
                sp.dma_start(xT_sb[:, n * UK:(n + 1) * UK, :], xT_v[:, n * UK:(n + 1) * UK, :]).then_inc(xT_in[n], 16)
                if n % 2 == 0:
                    load(n // 2)
            for u in (2, 3):
                load(u)
            sp.dma_start(rw, r_w.rearrange("n i j -> i n j")).then_inc(gate_w_in, 16)
            sp.dma_start(iw, i_w.rearrange("n i j -> i n j")).then_inc(gate_w_in, 16)
            for u in range(RAW, NU):
                load(u)
                if u == 3 * UPC - 1:
                    sp.dma_start(ident[:, :], identity).then_inc(ident_in, 16)
                    for n in range(4):
                        sp.dma_start(rope_t[:, n], rope_cs[n % 2]).then_inc(table_in, 16)
                    for n in range(2):
                        sp.dma_start(head_norm[:, n], head_norms[n, :].partition_broadcast(P)).then_inc(table_in, 16)
                if u == C_B * UPC - 1:
                    sp.wait_ge(b_done, NB)
                    sp.dma_start(x_sb, x.rearrange("(t p) c -> p t c", p=P)).then_inc(x_in, 16)
            for n, (i, c0, c1) in enumerate(Y_PARTS):
                t, d = i % TT, i // TT
                sp.wait_ge(y_done, n + 1)
                sp.dma_start(y[t * P:(t + 1) * P, d * CH + c0:d * CH + c1], y_sb[:, i, c0:c1]).then_inc(out_done, 16)
            sp.wait_ge(out_done, 16 * len(Y_PARTS))

        def heads(ap):
            return ap.rearrange("p (h d) -> p h d", d=DH)

        def chunk_free(c):
            if c < 2:
                return x_done, 4 * (c + 1)
            if c < C_OUT_A:
                return g_done, 4 * (c - 1)
            if c < C_B:
                return o_done, 2 * (c - C_OUT_A + 1)
            return u_done, 2 * (c - C_B + 1)

        @block.gpsimd
        def _(pool):
            steps = [0]

            def step(ins):
                steps[0] += 1
                ins.then_inc(pool_step, 1)
                pool.wait_ge(pool_step, steps[0])

            nc.gpsimd.memset(ones[:, :], 1.0).then_inc(const_made, 1)
            step(nc.gpsimd.memset(mask_b[:, :], 0.0))
            nc.gpsimd.affine_select(out=mask_b[:, :], in_=mask_b[:, :], compare_op=ALU.is_ge, fill=NEG_INF, base=0,
                                    pattern=[[-1, P]], channel_multiplier=1).then_inc(const_made, 1)
            pool.wait_ge(atanh_ready, 1)
            step(nc.gpsimd.tensor_scalar(series, s2, 1.0 / 15, None, ALU.mult))
            for odd in (13, 11, 9, 7, 5, 3):
                step(nc.gpsimd.tensor_scalar(series, series, 1.0 / odd, None, ALU.add))
                step(nc.gpsimd.tensor_tensor(series, series, s2, ALU.mult))
            step(nc.gpsimd.tensor_scalar(series, series, 1.0, None, ALU.add))
            step(nc.gpsimd.tensor_tensor(series, series, s_, ALU.mult))
            nc.gpsimd.tensor_scalar(series, series, -RG_C, None, ALU.mult)
            step(nc.gpsimd.tensor_scalar(neg, neg, 0.0, -RG_C / 2, ALU.max, ALU.mult))
            step(nc.gpsimd.tensor_tensor(decay_half, series, neg, ALU.add))
            nc.gpsimd.tensor_scalar(decay_neg, decay_half, -0.5, None, ALU.mult).then_inc(lru_made, 1)
            pool.wait_ge(ident_in, 16)
            nc.gpsimd.tensor_copy(ident_b[:, :], ident[:, :]).then_inc(const_made, 1)
            pool.wait_ge(table_in, 16 * 6)
            half = DH // 2
            for n in range(2):
                for t in range(TT):
                    nc.gpsimd.tensor_tensor(rope_t[:, 2 * n, t, :], rope_t[:, 2 * n, t, :], head_norm[:, n], ALU.mult)
                    nc.gpsimd.tensor_tensor(rope_t[:, 2 * n + 1, t, 0:half], rope_t[:, 2 * n + 1, t, 0:half],
                                            head_norm[:, n, half:DH], ALU.mult)
                    nc.gpsimd.tensor_tensor(rope_t[:, 2 * n + 1, t, half:DH], rope_t[:, 2 * n + 1, t, half:DH],
                                            head_norm[:, n, 0:half], ALU.mult).then_inc(table_made, 1)
            for b in range(NB):
                pool.wait_ge(m_done, b // 2 + 1)
                pool.wait_ge(ia_done, b + 1)
                nc.gpsimd.tensor_tensor(igate[:, b, :], igate[:, b, :], drive[:, b, :], ALU.mult).then_inc(b_done, 1)

        @block.scalar
        def _(act):
            def split_hi(u):
                c, ks, cs = unit(u)
                act.wait_ge(raw_in[u % RAW], 16 * (u // RAW + 1))
                if c >= WR:
                    act.wait_ge(*chunk_free(c - WR))
                gamma = CHUNKS[c][1]
                if gamma is None:
                    nc.scalar.activation(w_hi[:, c % WR, ks, cs], raw_unit(u), ACT.Copy).then_inc(hi_done, 1)
                else:
                    for k in range(UK):
                        last = nc.scalar.activation(w_hi[:, c % WR, ks.start + k, :], raw_unit(u)[:, k], ACT.Copy,
                                                    scale=V(gamma)[:, ks.start + k:ks.start + k + 1])
                    last.then_inc(hi_done, 1)

            def inv_sqrt(ready, count, ms, out, done):
                act.wait_ge(ready, count)
                nc.scalar.activation(out, ms, ACT.Ln).then_inc(done, 1)
                act.wait_ge(done, 2 * count - 1)
                nc.scalar.activation(out, out, ACT.Exp, scale=-0.5).then_inc(done, 1)

            nc.scalar.preload_act_table_set("natural_log_exp_and_others")
            act.wait_ge(lam_abs, 1)
            nc.scalar.activation(e, mag, ACT.Exp, scale=-1.0).then_inc(lam_exp, 1)
            for n in range(UPC):
                act.wait_ge(xT_in[n], 16)
                for k in (2 * n, 2 * n + 1):
                    last = nc.scalar.activation(act_hi[:, k, :], xT_sb[:, k, :], ACT.Copy, scale=V("a_norm")[:, k:k + 1])
                last.then_inc(hhi_done, 1)
                nc.scalar.activation(square[:, n * UK:(n + 1) * UK, :], xT_sb[:, n * UK:(n + 1) * UK, :],
                                     ACT.Square).then_inc(squared, 1)
                if n % 2 == 0:
                    split_hi(n // 2)
            split_hi(2)
            split_hi(3)
            inv_sqrt(ms0_done, 1, ms0, y0, y0_done)
            nc.scalar.preload_act_table_set("exp_and_others")

            def gates(b):
                pri = bank[4 + b % 2]
                act.wait_ge(ri_done, b + 1)
                if b == 0:
                    act.wait_ge(lru_made, 1)
                nc.scalar.activation(rgate[:, b, :], pri[:, 0:S], ACT.Tanh, scale=0.5,
                                     bias=rb_half[:, b:b + 1]).then_inc(gates_done, 1)
                nc.scalar.activation(igate[:, b, :], pri[:, S:2 * S], ACT.Tanh, scale=0.5,
                                     bias=ib_half[:, b:b + 1]).then_inc(gates_done, 1)
                act.wait_ge(gates_done, 2 * b + 1)
                nc.scalar.activation(decay[:, b, :], rgate[:, b, :], ACT.Exp, scale=decay_half[:, b:b + 1],
                                     bias=decay_half[:, b:b + 1]).then_inc(decay_done, 1)
                nc.scalar.activation(drive[:, b, :], rgate[:, b, :], ACT.Tanh, scale=decay_neg[:, b:b + 1],
                                     bias=decay_neg[:, b:b + 1]).then_inc(decay_done, 1)

            def mix_part_hi(p):
                act.wait_ge(mix_done, 2 * p + 2)
                nc.scalar.activation(mix_hi[:, 2 * p:2 * p + 2, :], mix[:, 2 * p:2 * p + 2, :],
                                     ACT.Copy).then_inc(mhi_done, 1)

            def x1T_hi(i):
                t, d = i % TT, i // TT
                act.wait_ge(xt_done, i + 1)
                nc.scalar.activation(act_hi[:, 4 * d:4 * d + 4, t * P:(t + 1) * P], heads(turn_bank("x1T", i)[:, :]),
                                     ACT.Copy).then_inc(xhi_done, 1)

            def tap0(b):
                act.wait_ge(xs_done, b + 1)
                nc.scalar.activation(conv[:, b, :], xs[:, b, :], ACT.Identity, scale=V("conv_w3")[:, b:b + 1],
                                     bias=V("conv_b")[:, b:b + 1]).then_inc(tap0_done, 1)

            def sqrt_parts(_):
                act.wait_ge(decay_done, 2 * NB)
                for p in range(NB // 2):
                    nc.scalar.activation(drive[:, 2 * p:2 * p + 2, :], drive[:, 2 * p:2 * p + 2, :], ACT.Sqrt,
                                         scale=0.25).then_inc(m_done, 1)
                nc.scalar.preload_act_table_set("silu_and_others")

            def silu_gate(b):
                act.wait_ge(zs_done, b + 1)
                act.wait_ge(scan_done, b + 1)
                nc.scalar.activation(silu_z[:, b, :], zs[:, b, :], ACT.Silu).then_inc(silu_done, 1)

            for what, arg in steps_of(ACT_G):
                {"split": split_hi, "tap": tap0, "gates": gates, "sqrt": sqrt_parts, "silu": silu_gate, "mix": mix_part_hi}[what](arg)
            nc.scalar.preload_act_table_set("natural_log_exp_and_others")

            def x1_squares(i):
                t, d = i % TT, i // TT
                act.wait_ge(x1_done, i + 1)
                if i >= 1:
                    act.wait_ge(x1sq_done, i)
                nc.scalar.activation(sq_sb, x1[:, t, d * CH:(d + 1) * CH], ACT.Square,
                                     accum_out=ssq[:, t, d:d + 1]).then_inc(x1sq_done, 1)

            for what, arg in steps_of(ACT_O):
                {"split": split_hi, "sq": x1_squares, "xT": x1T_hi,
                 "rms1": lambda _: inv_sqrt(ms1_done, 1, ms1, rstd1, y1_done)}[what](arg)

            def kqT_copy(kq):
                dst = (keyT, queryT)[kq % 2]
                for t in range(TT):
                    i = 2 * kq + t
                    act.wait_ge(t_done, i + 1)
                    nc.scalar.activation(dst[:, HG * (kq // 2):HG * (kq // 2 + 1), t * P:(t + 1) * P],
                                         heads(turn_bank("kqT", i)[:, :]), ACT.Copy).then_inc(tcopy_done, 1)

            def exps(h):
                act.wait_ge(nb_done, h + 1)
                if h >= 2:
                    act.wait_ge(pt_done, h - 1)
                sc = bank[6 + h % 2]
                nc.scalar.activation(prob[:, h % 2, 0:P], sc[:, 0:P], ACT.Exp, scale=q_scale[:, 0, h:h + 1],
                                     bias=nbias[:, 0, h:h + 1], accum_out=psum_l[:, h, 0:1])
                nc.scalar.activation(prob[:, h % 2, P:3 * P], sc[:, P:3 * P], ACT.Exp, scale=q_scale[:, 1, h:h + 1],
                                     bias=nbias[:, 1, h:h + 1], accum_out=psum_l[:, h, 1:2]).then_inc(p_done, 1)
                if h == H - 1:
                    nc.scalar.preload_act_table_set("silu_and_others")

            def oT_hi(i):
                t, g = i % TT, i // TT
                act.wait_ge(ot_done, i + 1)
                nc.scalar.activation(mix_hi[:, HG * g:HG * (g + 1), t * P:(t + 1) * P], heads(turn_bank("oT", i)[:, :]),
                                     ACT.Copy).then_inc(mhi_done, 1)

            def way_out(n):
                t, kind, acc = n % TT, KINDS[n // TT], bank[n % 3]
                act.wait_ge(u_done, n + 1)
                if kind in "kq":
                    m = earlier(n, "kq")
                    if n == 0:
                        act.wait_ge(rstd1_done, 1)
                    if t == 0 and m:
                        act.wait_ge(msk_done, m // 2)
                    for h in range(HG):
                        if m or h:
                            act.wait_ge(sq_done, HG * m + h)
                        nc.scalar.activation(sq_sb[:, 0:DH], acc[:, h * DH:(h + 1) * DH], ACT.Square, scale=rstd1[:, t:t + 1],
                                             accum_out=ssk[:, HG * t + h:HG * t + h + 1]).then_inc(sq_done, 1)
                elif kind == "v":
                    nc.scalar.activation(value[:, t, HALF[n // TT] * CH:(HALF[n // TT] + 1) * CH], acc[:, :], ACT.Copy,
                                         scale=rstd1[:, t:t + 1]).then_inc(v_done, 1)
                else:
                    m = earlier(n, "g")
                    if m == 0:
                        act.wait_ge(kq_done, 4)
                    if m >= 2:
                        act.wait_ge(og_done, m - 1)
                    nc.scalar.activation(gate[:, m % 2], acc[:, :], ACT.Silu, scale=rstd1[:, t:t + 1]).then_inc(gate_done, 1)

            def rms(kq):
                inv_sqrt(msk_done, kq + 1, msk, nyk, yk_done)

            for what, arg in steps_of(ACT_B):
                {"out": way_out, "split": split_hi, "rms": rms, "kqT": kqT_copy, "exp": exps, "oT": oT_hi}[what](arg)

        @block.vector
        def _(dve):
            steps = [0]

            def step(ins):
                steps[0] += 1
                ins.then_inc(dve_step, 1)
                dve.wait_ge(dve_step, steps[0])

            def split_lo(u):
                c, ks, cs = unit(u)
                dve.wait_ge(hi_done, u + 1)
                gamma = CHUNKS[c][1]
                if gamma is None:
                    last = nc.vector.tensor_tensor(w_lo[:, c % WR, ks, cs], raw_unit(u),
                                                   w_hi[:, c % WR, ks, cs].bitcast(F32), ALU.subtract)
                else:
                    for k in range(UK):
                        last = nc.vector.scalar_tensor_tensor(w_lo[:, c % WR, ks.start + k, :], raw_unit(u)[:, k],
                                                              V(gamma)[:, ks.start + k:ks.start + k + 1],
                                                              w_hi[:, c % WR, ks.start + k, :].bitcast(F32), ALU.mult, ALU.subtract)
                last.then_inc(lo_done, 1)

            def refine(y, ms, t, out):
                step(nc.vector.tensor_tensor(t, y, y, ALU.mult))
                step(nc.vector.scalar_tensor_tensor(t, t, -0.5, ms, ALU.mult, ALU.mult))
                return nc.vector.scalar_tensor_tensor(out, t, 1.5, y, ALU.add, ALU.mult)

            dve.wait_ge(vec_in, 16)
            step(nc.vector.tensor_scalar(neg, V("lambda"), -1.0, None, ALU.mult))
            nc.vector.tensor_tensor(mag, V("lambda"), neg, ALU.max).then_inc(lam_abs, 1)
            step(nc.vector.tensor_scalar(rb_half, V("r_b"), 0.5, None, ALU.mult))
            step(nc.vector.tensor_scalar(ib_half, V("i_b"), 0.5, None, ALU.mult))
            dve.wait_ge(lam_exp, 1)
            step(nc.vector.tensor_scalar(s2, e, 2.0, None, ALU.add))
            step(nc.vector.reciprocal(s_, s2))
            step(nc.vector.tensor_tensor(s_, e, s_, ALU.mult))
            nc.vector.tensor_tensor(s2, s_, s_, ALU.mult).then_inc(atanh_ready, 1)
            for n in range(UPC):
                dve.wait_ge(hhi_done, n + 1)
                for k in (2 * n, 2 * n + 1):
                    last = nc.vector.scalar_tensor_tensor(act_lo[:, k, :], xT_sb[:, k, :], V("a_norm")[:, k:k + 1],
                                                          act_hi[:, k, :].bitcast(F32), ALU.mult, ALU.subtract)
                last.then_inc(hlo_done, 1)
                if n % 2 == 0:
                    split_lo(n // 2)
            dve.wait_ge(stat_done, 1)
            nc.vector.tensor_scalar(ms0, bank[6][:, 0:S], 1.0 / D, EPS, ALU.mult, ALU.add).then_inc(ms0_done, 1)
            split_lo(2)
            dve.wait_ge(y0_done, 2)
            refine(y0, ms0, nt0, rstd0).then_inc(rstd0_done, 1)
            dve.wait_ge(rstd0_done, 1)

            def scale_x(b):
                dve.wait_ge(x_done, b + 1)
                nc.vector.tensor_tensor(xs[:, b, :], bank[b % 4][:, 0:S], rstd0, ALU.mult).then_inc(xs_done, 1)

            scale_x(0)
            split_lo(3)

            def convolve(n):
                b, back = n // 3, n % 3 + 1
                if back == 1:
                    dve.wait_ge(tap0_done, b + 1)
                else:
                    dve.wait_ge(conv_done, n)
                nc.vector.scalar_tensor_tensor(conv[:, b, back:S], xs[:, b, 0:S - back], V(f"conv_w{3 - back}")[:, b:b + 1],
                                               conv[:, b, back:S], ALU.mult, ALU.add).then_inc(conv_done, 1)

            def recur(b):
                dve.wait_ge(b_done, b + 1)
                nc.vector.tensor_tensor_scan(state[:, b, :], decay[:, b, :], igate[:, b, :], 0.0, ALU.mult,
                                             ALU.add).then_inc(scan_done, 1)

            def gate_out(b):
                dve.wait_ge(g_done, b + 1)
                dve.wait_ge(ix_done, b + 1)
                nc.vector.tensor_tensor(zs[:, b, :], bank[b % 4][:, 0:S], rstd0, ALU.mult).then_inc(zs_done, 1)

            def gate_mix(b):
                dve.wait_ge(silu_done, b + 1)
                dve.wait_ge(scan_done, b + 1)
                nc.vector.tensor_tensor(mix[:, b, :], silu_z[:, b, :], state[:, b, :], ALU.mult).then_inc(mix_done, 1)

            def gated_x(b):
                dve.wait_ge(gates_done, 2 * b + 2)
                nc.vector.scalar_tensor_tensor(igate[:, b, :], igate[:, b, :], 1.0, conv[:, b, :], ALU.add,
                                               ALU.mult).then_inc(ix_done, 1)

            def one_plus_decay(b):
                dve.wait_ge(ix_done, b + 1)
                dve.wait_ge(decay_done, 2 * b + 1)
                nc.vector.scalar_tensor_tensor(igate[:, b, :], decay[:, b, :], 1.0, igate[:, b, :], ALU.add,
                                               ALU.mult).then_inc(ia_done, 1)

            def mix_part_lo(p):
                dve.wait_ge(mhi_done, p + 1)
                nc.vector.tensor_tensor(mix_lo[:, 2 * p:2 * p + 2, :], mix[:, 2 * p:2 * p + 2, :],
                                        mix_hi[:, 2 * p:2 * p + 2, :].bitcast(F32), ALU.subtract).then_inc(mlo_done, 1)

            for what, arg in steps_of(DVE_G):
                {"split": split_lo, "xs": scale_x, "conv": convolve, "ix": gated_x, "ia": one_plus_decay, "zs": gate_out,
                 "scan": recur, "mix": gate_mix, "lo": mix_part_lo}[what](arg)

            def x1T_lo(i):
                t, d = i % TT, i // TT
                dve.wait_ge(xhi_done, i + 1)
                nc.vector.tensor_tensor(act_lo[:, 4 * d:4 * d + 4, t * P:(t + 1) * P], heads(turn_bank("x1T", i)[:, :]),
                                        act_hi[:, 4 * d:4 * d + 4, t * P:(t + 1) * P].bitcast(F32),
                                        ALU.subtract).then_inc(xlo_done, 1)

            def add_x1(i):
                t, d = i % TT, i // TT
                dve.wait_ge(o_done, i + 1)
                if i == 0:
                    dve.wait_ge(scan_done, NB)
                    dve.wait_ge(x_in, 16)
                nc.vector.tensor_tensor(x1[:, t, d * CH:(d + 1) * CH], bank[O_BANKS[i]][:, :], x_sb[:, t, d * CH:(d + 1) * CH],
                                        ALU.add).then_inc(x1_done, 1)

            def x1_rms(_):
                dve.wait_ge(x1sq_done, 4)
                step(nc.vector.tensor_tensor(ms1, ssq[:, :, 0], ssq[:, :, 1], ALU.add))
                nc.vector.tensor_scalar(ms1, ms1, 1.0 / D, EPS, ALU.mult, ALU.add).then_inc(ms1_done, 1)
                dve.wait_ge(ms1_done, 1)
                dve.wait_ge(y1_done, 2)
                refine(rstd1, ms1, nt1, rstd1).then_inc(rstd1_done, 1)

            for what, arg in steps_of(DVE_O):
                {"split": split_lo, "x1": add_x1, "xT": x1T_lo, "rms1": x1_rms}[what](arg)

            def norm_rope(kq):
                slot = roped[kq % 2]
                dve.wait_ge(msk_done, kq + 1)
                dve.wait_ge(yk_done, 2 * kq + 2)
                step(refine(nyk, msk, ntk, nyk))
                y3 = nyk.rearrange("p (t h) -> p t h", t=TT)
                n3 = ntk.rearrange("p (t h) -> p t h", t=TT)
                r1 = rstd1.unsqueeze(2).to_broadcast([P, TT, HG])
                dve.wait_ge(add_done, 2 * kq + 2)
                if kq % 2 == 0:
                    step(nc.vector.tensor_tensor(n3, y3, r1, ALU.mult))
                    for t in range(TT):
                        last = nc.vector.tensor_tensor(heads(slot[:, t]), heads(slot[:, t]),
                                                       n3[:, t].unsqueeze(2).to_broadcast([P, HG, DH]), ALU.mult)
                    last.then_inc(kq_done, 1)
                else:
                    g = kq // 2
                    q_heads = slice(HG * g, HG * (g + 1))
                    step(nc.vector.scalar_tensor_tensor(q_scale[:, :, q_heads], y3, SCALE, r1, ALU.mult, ALU.mult))
                    nc.vector.tensor_scalar(q_nscale[:, :, q_heads], q_scale[:, :, q_heads], -1.0, None, ALU.mult).then_inc(kq_done, 1)

            def mean_square(kq):
                dve.wait_ge(sq_done, 2 * HG * (kq + 1))
                nc.vector.tensor_scalar(msk, ssk, 1.0 / DH, EPS, ALU.mult, ALU.add).then_inc(msk_done, 1)

            def maxima(h):
                sc = bank[6 + h % 2]
                dve.wait_ge(s_done, h + 1)
                nc.vector.reduce_max(smax[:, 0, h:h + 1], sc[:, 0:P], AX_X)
                step(nc.vector.reduce_max(smax[:, 1, h:h + 1], sc[:, P:3 * P], AX_X))
                nc.vector.tensor_tensor(nbias[:, :, h], smax[:, :, h], q_nscale[:, :, h], ALU.mult).then_inc(nb_done, 1)

            def probT_copy(h):
                dve.wait_ge(pt_done, h + 1)
                if h >= 2:
                    dve.wait_ge(pv_done, h - 1)
                nc.vector.tensor_copy(probT[:, h % 2], turn_bank("pT", h)[:, 0:3 * P]).then_inc(ptc_done, 1)

            def attend(u):
                g, h0 = 2 * u // HG, 2 * u % HG
                dve.wait_ge(pv_done, 2 * u + 2)
                step(nc.vector.reciprocal(recip_l[:, 2 * u:2 * u + 2, :], psum_l[:, 2 * u:2 * u + 2, :]))
                for hh in range(2):
                    last = nc.vector.tensor_tensor(att[g][:, :, (h0 + hh) * DH:(h0 + hh + 1) * DH],
                                                   bank[3][:, hh * 2 * P:(hh + 1) * 2 * P].rearrange("p (t d) -> p t d", t=TT),
                                                   recip_l[:, 2 * u + hh, :].unsqueeze(2).to_broadcast([P, TT, DH]), ALU.mult)
                last.then_inc(on_done, 1)

            def oT_lo(i):
                t, g = i % TT, i // TT
                dve.wait_ge(mhi_done, NB // 2 + i + 1)
                nc.vector.tensor_tensor(mix_lo[:, HG * g:HG * (g + 1), t * P:(t + 1) * P], heads(turn_bank("oT", i)[:, :]),
                                        mix_hi[:, HG * g:HG * (g + 1), t * P:(t + 1) * P].bitcast(F32),
                                        ALU.subtract).then_inc(mlo_done, 1)

            def way_out(n):
                t, kind, acc = n % TT, KINDS[n // TT], bank[n % 3]
                if kind in "kq":
                    m = earlier(n, "kq")
                    kq = m // 2
                    slot = roped[kq % 2]
                    table = 2 * (kq % 2)
                    half = DH // 2
                    if m == 0:
                        dve.wait_ge(table_made, 4)
                    else:
                        dve.wait_ge(add_done, m)
                    dve.wait_ge(sq_done, HG * (m + 1))
                    if kq >= 2:
                        dve.wait_ge(t_done, 2 * (kq - 1))
                    nc.vector.tensor_tensor(heads(slot[:, t]), heads(acc[:, :]),
                                            rope_t[:, table, t].unsqueeze(1).to_broadcast([P, HG, DH]), ALU.mult)
                    for to, fro in ((0, half), (half, 0)):
                        sine = rope_t[:, table + 1, t, to:to + half].unsqueeze(1).to_broadcast([P, HG, half])
                        last = nc.vector.tensor_tensor(heads(swap_sb)[:, :, to:to + half],
                                                       heads(acc[:, :])[:, :, fro:fro + half], sine, ALU.mult)
                    last.then_inc(cos_done, 1)
                    dve.wait_ge(cos_done, m + 1)
                    nc.vector.tensor_tensor(slot[:, t], slot[:, t], swap_sb, ALU.add).then_inc(add_done, 1)

            def gate_attention(m):
                t, g = m % TT, m // TT
                dve.wait_ge(gate_done, m + 1)
                dve.wait_ge(on_done, 2 * (g + 1))
                nc.vector.tensor_tensor(att[g][:, t], gate[:, m % 2], att[g][:, t], ALU.mult).then_inc(og_done, 1)

            for what, arg in steps_of(DVE_B):
                {"out": way_out, "split": split_lo, "ms": mean_square, "norm": norm_rope, "max": maxima,
                 "probT": probT_copy, "attend": attend, "gate": gate_attention, "oT": oT_lo}[what](arg)

            for n, (i, c0, c1) in enumerate(Y_PARTS):
                t, d = i % TT, i // TT
                dve.wait_ge(f_done, n + 1)
                nc.vector.tensor_tensor(y_sb[:, i, c0:c1], y_bank(i, c0)[:, c0:c1], x1[:, t, d * CH + c0:d * CH + c1],
                                        ALU.add).then_inc(y_done, 1)

        @block.tensor
        def _(pe):
            def product(out, a_hi, a_lo, w, start, stop):
                nc.tensor.matmul(out, a_hi, w[0], start=start, stop=False)
                nc.tensor.matmul(out, a_hi, w[1], start=False, stop=False)
                return nc.tensor.matmul(out, a_lo, w[0], start=False, stop=stop)

            def weights_ready(c, k):
                if k % UK == 0:
                    pe.wait_ge(lo_done, UPC * c + k // UK + 1)

            pe.wait_ge(const_made, 1)
            for _ in range(WARM):
                nc.tensor.matmul(bank[7][:, 0:P], ones[:, :], ones[:, :], start=True, stop=True)

            def channels(c, b, done, first, gates_at):
                cols_ = slice((b % 4) * P, (b % 4 + 1) * P)
                out = bank[b % 4][:, 0:S]
                for k in range(KT):
                    if k in gates_at:
                        gate_products(gates_at[k])
                    if first and k % UK == 0:
                        for n in {0: (0, 1), UK: (2,), 2 * UK: (3,)}.get(k, ()):
                            pe.wait_ge(squared, n + 1)
                            for j in range(n * UK, (n + 1) * UK):
                                last = nc.tensor.matmul(bank[6][:, 0:S], ones[:, :], square[:, j, :], start=(j == 0),
                                                        stop=(j == KT - 1))
                            if j == KT - 1:
                                last.then_inc(stat_done, 1)
                        pe.wait_ge(hlo_done, k // UK + 1)
                    if c == 0:
                        if b % 2 == 0 and k % (2 * UK) == 0:
                            pe.wait_ge(lo_done, b + k // (2 * UK) + 1)
                    elif b % 4 == 0:
                        weights_ready(c, k)
                    wh, wl = w_hi[:, c % WR, k, cols_], w_lo[:, c % WR, k, cols_]
                    nc.tensor.matmul(out, wh, act_hi[:, k, :], start=(k == 0), stop=False)
                    nc.tensor.matmul(out, wh, act_lo[:, k, :], start=False, stop=False)
                    last = nc.tensor.matmul(out, wl, act_hi[:, k, :], start=False, stop=(k == KT - 1))
                last.then_inc(done, 1)

            def gate_products(b):
                pri = bank[4 + b % 2]
                pe.wait_ge(conv_done, 3 * b + 3)
                if b == 0:
                    pe.wait_ge(gate_w_in, 32)
                if b >= 2:
                    pe.wait_ge(gates_done, 2 * (b - 1))
                nc.tensor.matmul(pri[:, 0:S], rw[:, b, :], conv[:, b, :], start=True, stop=True)
                nc.tensor.matmul(pri[:, S:2 * S], iw[:, b, :], conv[:, b, :], start=True, stop=True).then_inc(ri_done, 1)

            for b in range(NB):
                if b >= 4:
                    pe.wait_ge(xs_done, b - 3)
                channels(b // 4, b, x_done, b == 0, GATES_AT.get(b, {}))
            for b in range(NB):
                if b < 4:
                    pe.wait_ge(xs_done, b + 5)
                else:
                    pe.wait_ge(zs_done, b - 3)
                channels(2 + b // 4, b, g_done, False, GATES_AT.get(NB + b, {}))

            def x1_turn(i):
                t, d = i % TT, i // TT
                out = turn_bank("x1T", i)
                pe.wait_ge(x1_done, i + 1)
                pe.wait_ge(*turn_free("x1T", i))
                if i == 0:
                    pe.wait_ge(ident_in, 16)
                for k in range(4):
                    last = nc.tensor.transpose(out[:, k * P:(k + 1) * P], x1[:, t, d * CH + k * P:d * CH + (k + 1) * P],
                                               ident[:, :])
                last.then_inc(xt_done, 1)

            for i, k0, k1 in ((0, 0, 4), (1, 0, 4), (0, 4, 6), (1, 4, 6), (0, 6, 8), (1, 6, 8), (2, 0, 8), (3, 0, 8)):
                t, d = i % TT, i // TT
                c = C_OUT_A + d
                if k0 == 0 and i >= 2:
                    pe.wait_ge(zs_done, 4 + O_BANKS[i] + 1)
                for k in range(k0, k1):
                    if (i, k) in X1_TURN_AT:
                        x1_turn(X1_TURN_AT[i, k])
                    if t == 0:
                        weights_ready(c, k)
                    if i == 0 and k % 2 == 0:
                        pe.wait_ge(mlo_done, k // 2 + 1)
                    last = product(bank[O_BANKS[i]][:, :], mix_hi[:, k, t * P:(t + 1) * P], mix_lo[:, k, t * P:(t + 1) * P],
                                   (w_hi[:, c % WR, k, :], w_lo[:, c % WR, k, :]), k == 0, k == KT - 1)
                if k1 == KT:
                    last.then_inc(o_done, 1)

            def kq_turn(kq):
                slot = roped[kq % 2]
                pe.wait_ge(kq_done, kq + 1)
                for t in range(TT):
                    i = 2 * kq + t
                    pe.wait_ge(*turn_free("kqT", i))
                    for h in range(HG):
                        last = nc.tensor.transpose(turn_bank("kqT", i)[:, h * P:(h + 1) * P], slot[:, t, h * DH:(h + 1) * DH],
                                                   ident[:, :])
                    last.then_inc(t_done, 1)

            def scores(h):
                sc = bank[6 + h % 2]
                pe.wait_ge(tcopy_done, 4 * (h // HG + 1))
                if h == 0:
                    pe.wait_ge(const_made, 3)
                if h >= 2:
                    pe.wait_ge(p_done, h - 1)
                nc.tensor.matmul(sc[:, 0:P], queryT[:, h, 0:P], keyT[:, h, 0:P], start=True, stop=False)
                nc.tensor.matmul(sc[:, 0:P], ident_b[:, :], mask_b[:, :], start=False, stop=True)
                nc.tensor.matmul(sc[:, P:3 * P], queryT[:, h, P:2 * P], keyT[:, h, 0:2 * P], start=True, stop=False)
                nc.tensor.matmul(sc[:, 2 * P:3 * P], ident_b[:, :], mask_b[:, :], start=False, stop=True).then_inc(s_done, 1)

            def prob_turn(h):
                pe.wait_ge(p_done, h + 1)
                pe.wait_ge(*turn_free("pT", h))
                for i in range(3):
                    last = nc.tensor.transpose(turn_bank("pT", h)[:, i * P:(i + 1) * P], prob[:, h % 2, i * P:(i + 1) * P],
                                               ident[:, :])
                last.then_inc(pt_done, 1)

            def weighted_values(h):
                pe.wait_ge(ptc_done, h + 1)
                pe.wait_ge(v_done, 2 * (h // HG + 1))
                if h == 0:
                    pe.wait_ge(x1_done, 4)
                elif h % 2 == 0:
                    pe.wait_ge(on_done, h // 2)
                at = (h % 2) * 2 * P
                pT = probT[:, h % 2]
                v = [value[:, t, h * DH:(h + 1) * DH] for t in range(TT)]
                nc.tensor.matmul(bank[3][:, at:at + P], pT[:, 0:P], v[0], start=True, stop=True)
                nc.tensor.matmul(bank[3][:, at + P:at + 2 * P], pT[:, P:2 * P], v[0], start=True, stop=False)
                nc.tensor.matmul(bank[3][:, at + P:at + 2 * P], pT[:, 2 * P:3 * P], v[1], start=False, stop=True).then_inc(pv_done, 1)

            def mix_turn(i):
                t, g = i % TT, i // TT
                pe.wait_ge(og_done, i + 1)
                pe.wait_ge(*turn_free("oT", i))
                for h in range(HG):
                    last = nc.tensor.transpose(turn_bank("oT", i)[:, h * P:(h + 1) * P], att[g][:, t, h * DH:(h + 1) * DH],
                                               ident[:, :])
                last.then_inc(ot_done, 1)

            small_steps = {"kqT": kq_turn, "scores": scores, "pT": prob_turn, "pv": weighted_values, "oT": mix_turn}

            def beside(n, k):
                for text in PE_B.get((n, k), []):
                    name, arg = text.split()
                    small_steps[name](int(arg))

            for n, k0, k1 in [(0, 0, 4), (1, 0, 4), (0, 4, 8), (1, 4, 8)] + [(n, 0, KT) for n in range(2, 16)]:
                t, c = n % TT, C_B + n // TT
                if k0 == 0:
                    pe.wait_ge(*acc_free(n))
                for k in range(k0, k1):
                    if (n, k) == (0, 3):
                        x1_turn(3)
                    beside(n, k)
                    if t == 0:
                        weights_ready(c, k)
                    if n < 2 and k % 4 == 0:
                        pe.wait_ge(xlo_done, 2 * (k // 4) + t + 1)
                    last = product(bank[n % 3][:, :], act_hi[:, k, t * P:(t + 1) * P], act_lo[:, k, t * P:(t + 1) * P],
                                   (w_hi[:, c % WR, k, :], w_lo[:, c % WR, k, :]), k == 0, k == KT - 1)
                if k1 == KT:
                    last.then_inc(u_done, 1)

            for i, c0, c1 in Y_PARTS:
                t, d = i % TT, i // TT
                c = C_OUT_B + d
                if i < 3:
                    pe.wait_ge(*acc_free(16 + i))
                elif c0 == 0:
                    pe.wait_ge(y_done, 1)
                else:
                    pe.wait_ge(y_done, 2)
                for k in range(KT):
                    if c0 == 0:
                        beside(16 + i, k)
                    if t == 0:
                        weights_ready(c, k)
                    if i < 2 and k % 4 == 0:
                        pe.wait_ge(mlo_done, NB // 2 + 2 * (k // 4) + t + 1)
                    last = product(y_bank(i, c0)[:, c0:c1], mix_hi[:, k, t * P:(t + 1) * P], mix_lo[:, k, t * P:(t + 1) * P],
                                   (w_hi[:, c % WR, k, c0:c1], w_lo[:, c % WR, k, c0:c1]), k == 0, k == KT - 1)
                last.then_inc(f_done, 1)

    return nc


def kernel(**inputs):
    import numpy as np
    import concourse.bacc as bacc
    from concourse.bass_utils import run_bass_kernel_spmd

    a = {n: np.asarray(v) for n, v in inputs.items()}
    x = a["x"][0]
    S, D = x.shape
    DH = a["k_norm"].shape[0]
    half = DH // 2
    named = {"conv_b": a["a_conv_b"][0], "r_b": a["a_r_b"][0], "i_b": a["a_i_b"][0], "lambda": a["a_lambda"][0],
             "a_norm": a["a_norm"][0], "kv_norm": a["kv_norm"], "b_norm": a["b_norm"][0]}
    named.update({f"conv_w{k}": a["a_conv_w"][0, k] for k in range(4)})
    inv = np.float32(10000.0) ** (-np.arange(half, dtype=np.float32) / np.float32(half))
    angle = np.arange(S, dtype=np.float32)[:, None] * inv[None, :].astype(np.float32)
    cos, sin = np.cos(angle), np.sin(angle)
    table = np.stack([np.concatenate([cos, cos], 1), np.concatenate([-sin, sin], 1)]).astype(np.float32)
    arrays = {
        "xT": x.T, "x_rows": x, "in_w": a["a_in_w"][0], "r_w": a["a_r_w"][0], "i_w": a["a_i_w"][0],
        "a_out_w": a["a_out_w"][0], "kv_w": a["kv_w"], "b_in_w": a["b_in_w"][0], "b_out_w": a["b_out_w"][0],
        "vectors": np.stack([named[n].reshape(D // P, P).T for n in VECTORS], 1),
        "head_norms": np.stack([a["k_norm"], a["q_norm"][0]]),
        "rope_cs": table.reshape(2, S // P, P, DH).transpose(0, 2, 1, 3),
        "ident_in": np.eye(P, dtype=np.float32),
    }
    arrays = {n: np.ascontiguousarray(v) for n, v in arrays.items()}
    nc = bacc.Bacc("TRN2", target_bir_lowering=False, num_devices=1)
    args = [nc.dram_tensor(n, v.shape, mybir.dt.from_np(v.dtype), kind="ExternalInput").ap() for n, v in arrays.items()]
    y = nc.dram_tensor("y", (S, D), F32, kind="ExternalOutput").ap()
    hybrid_trunk(nc, *args, y)
    r = run_bass_kernel_spmd(nc, [arrays], core_ids=[0])
    return r.results[0]["y"].reshape(1, S, D)
```
